# Optimizing a Trainium2 kernel written in Bass

```python
import jax, jax.numpy as jnp
from jax import lax
import numpy as np

D_MODEL = 2048
BATCH = 1
SEQ = 256
DEPTH = 1

CTX_LEN = 256
GRID_W = 64
POOL_W = 1024
POOL_WINDOWS = (2, 4, 8, 16)
POOL_GROUP = POOL_W // len(POOL_WINDOWS)
GDN_HEADS = 8
GDN_DK = 128
GDN_DV = 128
GDN_W = GDN_HEADS * GDN_DV
CONV_W = 4
CONV_LEFT = 2
CHUNK = 64
D_FF = 5632
N_MOD = 9
EPS = 1e-6
COL_QKV = POOL_W
COL_Z = COL_QKV + 3 * GDN_W
COL_BA = COL_Z + GDN_W
IN_COLS = COL_BA + 4 * GDN_HEADS

kernel_name = "hybrid_pool_gdn_macaron_dit_block"

def rmsnorm(x, g):
    xf = x.astype(jnp.float32)
    y = xf * lax.rsqrt(jnp.mean(xf * xf, axis=-1, keepdims=True) + EPS)
    return (y * g.astype(jnp.float32)).astype(x.dtype)

def modulate(u, shift, scale):
    return u * (1 + scale[:, None]) + shift[:, None]

def swiglu(u, w_in, w_out):
    gate, up = jnp.split(u @ w_in, 2, axis=-1)
    return (jax.nn.silu(gate) * up) @ w_out

def pos_embed_2d(rows, cols, d):
    quarter = d // 4
    omega = 1.0 / (10000.0 ** (jnp.arange(quarter, dtype=jnp.float32) / quarter))
    t = jnp.arange(rows * cols)
    er = (t // cols).astype(jnp.float32)[:, None] * omega
    ec = (t % cols).astype(jnp.float32)[:, None] * omega
    return jnp.concatenate([jnp.sin(er), jnp.cos(er), jnp.sin(ec), jnp.cos(ec)], axis=-1)

def pool_mixer(u, w_pool, pool_scale):
    B, L, _ = u.shape
    uf = u.astype(jnp.float32)
    cs = jnp.concatenate([jnp.zeros_like(uf[:, :1]), jnp.cumsum(uf, axis=1)], axis=1)
    t = jnp.arange(L)
    outs = []
    for gi, w in enumerate(POOL_WINDOWS):
        lo_c, hi_c = gi * POOL_GROUP, (gi + 1) * POOL_GROUP
        lo = jnp.clip(t - w // 2, 0, L - 1)
        hi = jnp.clip(t + w // 2 - 1, 0, L - 1)
        csg = cs[..., lo_c:hi_c]
        win_sum = jnp.take(csg, hi + 1, axis=1) - jnp.take(csg, lo, axis=1)
        cnt = (hi - lo + 1).astype(jnp.float32)[None, :, None]
        outs.append(win_sum / cnt - uf[..., lo_c:hi_c])
    p = jnp.stack(outs, axis=2)
    y = jnp.einsum('blgc,gcd->blgd', p, w_pool.astype(jnp.float32)).reshape(B, L, POOL_W)
    return (y * pool_scale.astype(jnp.float32)).astype(u.dtype)

def short_conv(u, w):
    L = u.shape[1]
    up = jnp.pad(u, ((0, 0), (CONV_LEFT, CONV_W - 1 - CONV_LEFT), (0, 0)))
    return sum(up[:, j:j + L] * w[j] for j in range(CONV_W))

def l2norm(x):
    return x * lax.rsqrt(jnp.sum(x * x, axis=-1, keepdims=True) + EPS)

def gdn_prep(p, conv_w, a_log, dt_bias):
    B, L, _ = p.shape
    qkv = jax.nn.silu(short_conv(p[..., COL_QKV:COL_Z], conv_w)).astype(jnp.float32)
    qkv = qkv.reshape(B, L, 3, GDN_HEADS, GDN_DK)
    q = l2norm(qkv[:, :, 0]) * (GDN_DK ** -0.5)
    k = l2norm(qkv[:, :, 1])
    v = qkv[:, :, 2]
    ba = p[..., COL_BA:IN_COLS].astype(jnp.float32).reshape(B, L, 2, 2, GDN_HEADS)
    beta = jax.nn.sigmoid(ba[:, :, 0])
    g = -jnp.exp(a_log.astype(jnp.float32)) * jax.nn.softplus(ba[:, :, 1] + dt_bias.astype(jnp.float32))
    z = p[..., COL_Z:COL_BA]
    return q, k, v, g, beta, z

def chunk_gated_delta(q, k, v, g, beta, s0):
    B, L, H, _ = q.shape
    n = L // CHUNK

    def chunks(t):
        t = t.reshape((B, n, CHUNK, H) + t.shape[3:])
        return jnp.moveaxis(t, (1, 3), (0, 2))

    qc, kc, vc, gc, bc = chunks(q), chunks(k), chunks(v), chunks(g), chunks(beta)
    gc = jnp.cumsum(gc, axis=-1)
    tril = jnp.tril(jnp.ones((CHUNK, CHUNK), bool))
    strict = jnp.tril(jnp.ones((CHUNK, CHUNK), bool), -1)
    decay = jnp.exp(jnp.where(tril, gc[..., :, None] - gc[..., None, :], -jnp.inf))
    kb = kc * bc[..., None]
    vb = vc * bc[..., None]
    a_low = jnp.where(strict, jnp.einsum('nbhid,nbhjd->nbhij', kb, kc) * decay, 0.0)
    eye = jnp.eye(CHUNK, dtype=jnp.float32)
    rhs = jnp.concatenate([vb, kb * jnp.exp(gc)[..., None]], axis=-1)
    sol = lax.linalg.triangular_solve(eye + a_low, rhs, left_side=True, lower=True, unit_diagonal=True)
    u_val, w_kd = sol[..., :GDN_DV], sol[..., GDN_DV:]
    qk = jnp.einsum('nbhid,nbhjd->nbhij', qc, kc) * decay

    def step(S, xs):
        q_i, k_i, u_i, w_i, g_i, qk_i = xs
        v_new = u_i - jnp.einsum('bhck,bhkv->bhcv', w_i, S)
        o = (jnp.einsum('bhck,bhkv->bhcv', q_i * jnp.exp(g_i)[..., None], S)
             + jnp.einsum('bhij,bhjv->bhiv', qk_i, v_new))
        g_last = g_i[..., -1]
        S = (S * jnp.exp(g_last)[..., None, None]
             + jnp.einsum('bhck,bhcv->bhkv', k_i * jnp.exp(g_last[..., None] - g_i)[..., None], v_new))
        return S, o

    s_fin, o = lax.scan(step, s0, (qc, kc, u_val, w_kd, gc, qk))
    o = jnp.moveaxis(o, (0, 2), (1, 3)).reshape(B, L, H, GDN_DV)
    return o, s_fin

def gdn_direction(q, k, v, g, beta, s0, d):
    if d == 0:
        return chunk_gated_delta(q, k, v, g[:, :, 0], beta[:, :, 0], s0)
    fl = lambda t: jnp.flip(t, axis=1)
    o, s = chunk_gated_delta(fl(q), fl(k), fl(v), fl(g[:, :, 1]), fl(beta[:, :, 1]), s0)
    return fl(o), s

def gdn_gate_out(o, z, o_norm_g):
    B, L = o.shape[:2]
    on = o * lax.rsqrt(jnp.mean(o * o, axis=-1, keepdims=True) + EPS) * o_norm_g.astype(jnp.float32)
    zf = z.astype(jnp.float32).reshape(B, L, GDN_HEADS, GDN_DV)
    return (on * jax.nn.silu(zf)).reshape(B, L, GDN_W).astype(z.dtype)

def mixer_out(p, o, z, w_pool, pool_scale, o_norm_g, w_out):
    y = jnp.concatenate([pool_mixer(p[..., :POOL_W], w_pool, pool_scale),
                         gdn_gate_out(o, z, o_norm_g)], axis=-1)
    return y @ w_out

def setup_inputs(seed: int = 0) -> dict:
    key = jax.random.key(seed)
    ks = jax.random.split(key, 20)
    f32 = jnp.float32
    D = D_MODEL
    nrm = lambda k, s, sc: jax.random.normal(k, s, f32) * sc
    dt = jnp.exp(jax.random.uniform(ks[9], (DEPTH, 2, GDN_HEADS), f32, np.log(1e-3), np.log(1e-1)))
    return {
        "x": nrm(ks[0], (BATCH, SEQ, D), 1.0),
        "c": nrm(ks[1], (BATCH, D), 1.0),
        "ctx": nrm(ks[2], (BATCH, CTX_LEN, D), 1.0),
        "c_ctx": nrm(ks[3], (D,), 1.0),
        "w_ada": nrm(ks[4], (DEPTH, D, N_MOD * D), 0.3 * D ** -0.5),
        "b_ada": nrm(ks[5], (DEPTH, N_MOD * D), 0.01),
        "norm_g": 1.0 + nrm(ks[6], (DEPTH, 3, D), 0.05),
        "w_in": nrm(ks[7], (DEPTH, D, IN_COLS), D ** -0.5),
        "conv_w": nrm(ks[8], (DEPTH, CONV_W, 3 * GDN_W), CONV_W ** -0.5),
        "a_log": jnp.log(jax.random.uniform(ks[10], (DEPTH, 2, GDN_HEADS), f32, 1.0, 16.0)),
        "dt_bias": dt + jnp.log(-jnp.expm1(-dt)),
        "o_norm_g": 1.0 + nrm(ks[11], (DEPTH, GDN_DV), 0.05),
        "w_pool": nrm(ks[12], (DEPTH, len(POOL_WINDOWS), POOL_GROUP, POOL_GROUP), POOL_GROUP ** -0.5),
        "pool_scale": 1.0 + nrm(ks[13], (DEPTH, POOL_W), 0.1),
        "w_out": nrm(ks[14], (DEPTH, D, D), D ** -0.5),
        "ffn_w_in": nrm(ks[15], (DEPTH, 2, D, 2 * D_FF), D ** -0.5),
        "ffn_w_out": nrm(ks[16], (DEPTH, 2, D_FF, D), D_FF ** -0.5),
        "final_g": 1.0 + nrm(ks[17], (D,), 0.05),
    }

def reference(x, c, ctx, c_ctx, w_ada, b_ada, norm_g, w_in, conv_w, a_log, dt_bias, o_norm_g,
              w_pool, pool_scale, w_out, ffn_w_in, ffn_w_out, final_g):
    B, S, D = x.shape
    rows = S // GRID_W
    h = x + pos_embed_2d(rows, GRID_W, D).astype(x.dtype)[None]
    hc = ctx
    for li in range(DEPTH):
        ml = (jax.nn.silu(c) @ w_ada[li] + b_ada[li]).reshape(B, N_MOD, D)
        mc = (jax.nn.silu(c_ctx)[None] @ w_ada[li] + b_ada[li]).reshape(1, N_MOD, D)
        h = h + 0.5 * ml[:, 2][:, None] * swiglu(
            modulate(rmsnorm(h, norm_g[li, 0]), ml[:, 0], ml[:, 1]), ffn_w_in[li, 0], ffn_w_out[li, 0])
        hc = hc + 0.5 * mc[:, 2][:, None] * swiglu(
            modulate(rmsnorm(hc, norm_g[li, 0]), mc[:, 0], mc[:, 1]), ffn_w_in[li, 0], ffn_w_out[li, 0])
        pl = modulate(rmsnorm(h, norm_g[li, 1]), ml[:, 3], ml[:, 4]) @ w_in[li]
        pc = modulate(rmsnorm(hc, norm_g[li, 1]), mc[:, 3], mc[:, 4]) @ w_in[li]
        ql, kl, vl, gl, bl, zl = gdn_prep(pl, conv_w[li], a_log[li], dt_bias[li])
        qc, kc, vc, gc, bc, zc = gdn_prep(pc, conv_w[li], a_log[li], dt_bias[li])
        s0 = jnp.zeros((B, GDN_HEADS, GDN_DK, GDN_DV), jnp.float32)
        oc_f, sc_f = gdn_direction(qc, kc, vc, gc, bc, s0, 0)
        oc_b, sc_b = gdn_direction(qc, kc, vc, gc, bc, s0, 1)
        ol_f, _ = gdn_direction(ql, kl, vl, gl, bl, sc_f, 0)
        ol_b, _ = gdn_direction(ql, kl, vl, gl, bl, sc_b, 1)
        h = h + ml[:, 5][:, None] * mixer_out(pl, ol_f + ol_b, zl, w_pool[li], pool_scale[li],
                                              o_norm_g[li], w_out[li])
        h = h + 0.5 * ml[:, 8][:, None] * swiglu(
            modulate(rmsnorm(h, norm_g[li, 2]), ml[:, 6], ml[:, 7]), ffn_w_in[li, 1], ffn_w_out[li, 1])
        if li + 1 < DEPTH:
            hc = hc + mc[:, 5][:, None] * mixer_out(pc, oc_f + oc_b, zc, w_pool[li], pool_scale[li],
                                                    o_norm_g[li], w_out[li])
            hc = hc + 0.5 * mc[:, 8][:, None] * swiglu(
                modulate(rmsnorm(hc, norm_g[li, 2]), mc[:, 6], mc[:, 7]), ffn_w_in[li, 1], ffn_w_out[li, 1])
    return rmsnorm(h, final_g)


_drawn_inputs = setup_inputs


def setup_inputs(seed=0):
    import zlib

    import numpy as np

    out = dict(_drawn_inputs(seed))
    spreads = {}
    factors = {'ctx': 5.425,
     'c_ctx': 8.0,
     'b_ada': 8.0,
     'norm_g': 6.74,
     'a_log': 4.65,
     'dt_bias': 2.745,
     'o_norm_g': 8.0,
     'pool_scale': 6.762}
    for name, (base, spread) in spreads.items():
        noise = np.random.default_rng([zlib.crc32(name.encode()), seed]).standard_normal(out[name].shape)
        drawn = base * np.exp(spread * noise) if base else spread * noise
        out[name] = __import__('jax').numpy.asarray(drawn.astype(out[name].dtype))
    for name, factor in factors.items():
        out[name] = (out[name] * factor).astype(out[name].dtype)
    return out
```

```python
from contextlib import ExitStack

import numpy as np

import concourse.bass as bass
from concourse import mybir

F32 = mybir.dt.float32
F32R = mybir.dt.float32r
ALU = mybir.AluOpType
ACT = mybir.ActivationFunctionType
ds = bass.ds

P = 128
D = 2048
KT = D // P
SEQ = 256
NTOK = 2 * SEQ
D_FF = 5632
GRID_W = 64
POOL_W = 1024
POOL_WINDOWS = (2, 4, 8, 16)
POOL_GROUP = POOL_W // len(POOL_WINDOWS)
HEADS = 8
DK = 128
COL_QKV = POOL_W
COL_BA = COL_QKV + 4 * HEADS * DK
N_BA = 4 * HEADS
N_MOD = 9
CONV_W = 4
CONV_LEFT = 2
EPS = 1e-6

TILE_K = 2
TILE_N = 512
TILE = TILE_K * TILE_N
RAW = 8
HL = 4
AHEAD = HL - 1
K_TILES = KT // TILE_K

ADA_N = N_MOD * D // TILE_N
ADA_TILES = ADA_N * K_TILES

GROUP_FF = 4
GROUPS = D_FF // (GROUP_FF * P)
PAIRS = GROUP_FF // 2
N_OUT = D // TILE_N
OUT_TILES = GROUP_FF // TILE_K
GROUP_TILES = PAIRS * K_TILES + N_OUT * OUT_TILES

T_FFN1 = 0
T_HEADS = T_FFN1 + GROUPS * GROUP_TILES
T_POOL = T_HEADS + HEADS * K_TILES
T_WOUT = T_POOL + POOL_W // TILE_N * K_TILES
T_FFN2 = T_WOUT + N_OUT * K_TILES
T_END = T_FFN2 + GROUPS * GROUP_TILES


def transfers(t):
    if T_HEADS <= t < T_WOUT:
        return TILE_K
    base = T_FFN1 if t < T_HEADS else T_FFN2
    inside = base <= t and (t - base) % GROUP_TILES < PAIRS * K_TILES
    return TILE_K if inside else 1


LEVELS = (2, 4, 8, 16, 32, 64)
SCAN = ((2, 3, 0, 1), (3, 2, 1, 0))
BETA, G, GC, EG, NBEG, EGT, EKD = range(7)
PREP_G = 17


FAR = 1e4


def host_constants():
    quarter = D // 4
    omega = (1.0 / (10000.0 ** (np.arange(quarter, dtype=np.float32) / quarter))).astype(np.float32)
    t = np.arange(SEQ)
    er = (t // GRID_W).astype(np.float32)[:, None] * omega
    ec = (t % GRID_W).astype(np.float32)[:, None] * omega
    pos = np.concatenate([np.sin(er), np.cos(er), np.sin(ec), np.cos(ec)], axis=-1).astype(np.float32)
    i, j = np.arange(P)[:, None], np.arange(P)[None, :]
    ident = (i == j)
    levels = [((i // m) % 2 == 1) & (j // m == i // m - 1) for m in (1,) + LEVELS]
    masks = [FAR * (i <= j), FAR * (i >= j), i <= j, i >= j, np.ones((P, P))]
    masks += levels + [m.T for m in levels]
    masks = np.stack([m.astype(np.float32) for m in masks], axis=1).reshape(P, -1)
    pools = []
    for w in POOL_WINDOWS:
        lo, hi = np.clip(t - w // 2, 0, SEQ - 1), np.clip(t + w // 2 - 1, 0, SEQ - 1)
        inside = (t[None, :] >= lo[:, None]) & (t[None, :] <= hi[:, None])
        m = inside / (hi - lo + 1)[:, None] - np.eye(SEQ)
        pools.append(m.T.astype(np.float32))
    pools = np.stack(pools, axis=1)
    return {"pos": pos, "ident": ident.astype(np.float32), "masks": masks,
            "pools": np.ascontiguousarray(pools.reshape(SEQ, -1))}


MASKED, CUM, ONES, LEVEL = 0, 2, 4, 5
N_LEVEL = len(LEVELS) + 1
N_MASK = LEVEL + 2 * N_LEVEL


def build(nc, x, c, ctx, c_ctx, w_ada, b_ada, norm_g, w_in, conv_w, a_log, dt_bias, o_norm_g,
          w_pool, pool_scale, w_out, ffn_w_in, ffn_w_out, final_g, pos, ident_in, masks_in,
          pools_in, out):
    ada_rows = nc.dram_tensor("ada_rows", (2, N_MOD * D), F32, kind="Internal").ap()

    es = ExitStack()
    with es:
        def sb(name, shape, dt=F32, stack=es):
            return stack.enter_context(nc.sbuf_tensor(name, shape, dt))

        sems = {}

        def sem(name):
            sems[name] = es.enter_context(nc.semaphore(name))
            return sems[name]

        ps = es.enter_context(nc.psum_tensor("ps", [P, 8, 512], F32))

        xh = sb("xh", [P, KT, NTOK], F32R)
        xl = sb("xl", [P, KT, NTOK], F32R)
        h_lat = sb("h_lat", [P, 2, D])
        raw = sb("raw", [P, RAW, TILE])
        wh = sb("wh", [P, HL, TILE], F32R)
        wl = sb("wl", [P, HL, TILE], F32R)
        ident = sb("ident", [P, P])
        cols_a = sb("cols_a", [P, 128])
        cols_b = sb("cols_b", [P, 80])
        cols_c = sb("cols_c", [P, 105])
        scale_c = sb("scale_c", [P, 5, KT])
        n_ss = sb("n_ss", [P, 2])
        n_ms = sb("n_ms", [P, 2])
        n_rstd = sb("n_rstd", [P, 2])
        mhalf = sb("mhalf", [P, 8])

        with ExitStack() as st:
            h_ctx = sb("h_ctx", [P, 2, D], stack=st)
            gates = sb("gates", [P, 2, D], stack=st)
            sg = sb("sg", [P, 2, 512], stack=st)
            hf = sb("hf", [P, 2, 512], stack=st)
            tmp = sb("tmp", [P, 2, 512], stack=st)
            base_ht = ExitStack()
            with base_ht:
                hth = sb("hth", [P, GROUP_FF, 512], F32R, stack=base_ht)
                htl = sb("htl", [P, GROUP_FF, 512], F32R, stack=base_ht)
            with ExitStack() as first:
                crow = sb("crow", [32, P], stack=first)
                csil = sb("csil", [32, P], stack=first)
                cT = sb("cT", [P, 32], stack=first)
                brow = sb("brow", [2, 2, 512], stack=first)
                arow = sb("arow", [2, 2, 512], stack=first)
                rows_a = sb("rows_a", [128, P], stack=first)
                rows_b = sb("rows_b", [80, P], stack=first)
                rows_c = sb("rows_c", [105, P], stack=first)
            xn = sb("xn", [P, 2, D], stack=st)
            uk = xn[:].rearrange("p a b -> p (a b)").rearrange("p (k n) -> p k n", k=KT)
        yst = ExitStack()
        with yst:
            yg = sb("yg", [P, HEADS, SEQ], stack=yst)
            with ExitStack() as st:
                mk = sb("mk", [P, N_MASK, P], stack=st)
                gp = sb("gp", [P, 7, 4, 2 * HEADS], stack=st)
                hp = sb("hp", [P, 7, 4, 2], stack=st)
                cw = sb("cw", [P, 12], stack=st)
                pq = sb("pq", [P, SEQ + 4], stack=st)
                pk = sb("pk", [P, 2, SEQ + 4], stack=st)
                pv = sb("pv", [P, 2, SEQ + 4], stack=st)
                pz = sb("pz", [P, SEQ], stack=st)
                qT = sb("qT", [P, SEQ], stack=st)
                zs = sb("zs", [P, SEQ], stack=st)
                with ExitStack() as st2:
                    kT = sb("kT", [P, 2, SEQ], stack=st2)
                    vT = sb("vT", [P, 2, SEQ], stack=st2)
                AY = sb("AY", [P, 8, P], stack=st)
                with ExitStack() as st2:
                    wba = sb("wba", [P, KT, N_BA], stack=st2)
                    wbah = sb("wbah", [P, KT, N_BA], F32R, stack=st2)
                    wbal = sb("wbal", [P, KT, N_BA], F32R, stack=st2)
                    rowc = sb("rowc", [P, 2, 2 * HEADS], stack=st2)
                    sp_t = sb("sp_t", [P, 6, 4, 2 * HEADS], stack=st2)
                AT = sb("AT", [P, 8, P], stack=st)
                X = sb("X", [P, 8, P], stack=st)
                XT = sb("XT", [P, 8, P], stack=st)
                LE = sb("LE", [P, 8, P], stack=st)
                Aq = sb("Aq", [P, 4, P], stack=st)
                AqT = sb("AqT", [P, 4, P], stack=st)
                kh = sb("kh", [P, 4, P], stack=st)
                khT = sb("khT", [P, 4, P], stack=st)
                vb = sb("vb", [P, 8, P], stack=st)
                S, o, vbp, vn = (X[:, 2 * i:2 * i + 2, :] for i in range(4))
                ssb = sb("ssb", [P, 6], stack=st)
                rs = sb("rs", [P, 6], stack=st)
                rq = sb("rq", [P, 2], stack=st)
                oss = sb("oss", [P, 2], stack=st)
                oms = sb("oms", [P, 2], stack=st)
                ors = sb("ors", [P, 2], stack=st)
            with ExitStack() as st:
                u = sb("u", [P, 2, POOL_W], stack=st)
                pg = sb("pg", [P, 2, 4, SEQ], stack=st)
                pT = sb("pT", [P, 8, SEQ], stack=st)
                wp = sb("wp", [P, 4, 2, POOL_GROUP], stack=st)
                yp = sb("yp", [P, 8, SEQ], stack=st)

        raw_in = [sem(f"raw_in{i}") for i in range(RAW)]
        hi_done, lo_done, tile_used = sem("hi_done"), sem("lo_done"), sem("tile_used")
        ada_used, ada_evac = sem("ada_used"), sem("ada_evac")
        brow_in = [sem("brow_in0"), sem("brow_in1")]
        arow_out = [sem("arow_out0"), sem("arow_out1")]
        c_in, c_silu, c_turned, c_cols = sem("c_in"), sem("c_silu"), sem("c_turned"), sem("c_cols")
        id_in, x_in, pos_in = sem("id_in"), sem("x_in"), sem("pos_in")
        rows_in, rows_turned, cols_done, scale_done = (
            sem("rows_in"), sem("rows_turned"), sem("cols_done"), sem("scale_done"))
        rowsc_in, gates_in, gates_in2, fg_in = sem("rowsc_in"), sem("gates_in"), sem("gates_in2"), sem("fg_in")
        half_set, h_set = sem("half_set"), sem("h_set")
        ss_done, ms_done, rstd_done, xn_done, x_turned, u_done, uh_done, x_ready = (
            sem("ss_done"), sem("ms_done"), sem("rstd_done"), sem("xn_done"), sem("x_turned"),
            sem("u_done"), sem("uh_done"), sem("x_ready"))
        F = []
        for f in range(2):
            F.append({n: sem(f"{n}{f}") for n in ("silu_done", "hf_done", "hh_done", "h_ready")})
        gated = [sem(f"gated{i}") for i in range(3)]
        added = [sem(f"added{i}") for i in range(3)]
        out_done = sem("out_done")
        mk_in, ba_in, rowc_in = sem("mk_in"), sem("ba_in"), sem("rowc_in")
        ba_hi, ba_split, ba_done, prep_dve, prep_act, prep_pe = (
            sem("ba_hi"), sem("ba_split"), sem("ba_done"), sem("prep_dve"), sem("prep_act"), sem("prep_pe"))
        margins_set = sem("margins_set")
        pool_u, pool_p, pool_pe, pool_pe2, yp_done, y_hi, y_ready, pool_in = (
            sem("pool_u"), sem("pool_p"), sem("pool_pe"), sem("pool_pe2"), sem("yp_done"),
            sem("y_hi"), sem("y_ready"), sem("pool_in"))
        PER = dict(hp_set=1, cw_set=1, conv=12, act_in=4, squared=2, pe_v=1, pe_k=1, pe_ss=1,
                   ss_sb=1, rs_set=1, rq_set=1, kh_set=1, pe_kh=1, khT_set=1, vb_set=1, pe_g=1,
                   pe_cum=2, pe_qk=1, dd_set=2, e_set=2, ei_set=1, a_set=2, aq_set=1,
                   pe_at=2, pe_aqt=1, at_set=2, aqt_set=1, m1_set=2, mt_set=2, x1_set=4, lt_set=12,
                   pe_y=12, y_set=12, pe_zt=12, pe_z=10, x_set=10, xt_set=12, kd_set=2,
                   pe_r=6, vbp_set=6, pe_vn=8, vn_set=8, pe_kv=6, s_set=6, pe_av=4,
                   o_set=8, osc=1, oss_set=1, oms_set=1, ors_set=1, on_set=1, pe_o=1, y_done=1,
                   evac_act=2, evac_dve=2)
        HS = {n: sem("gdn_" + n) for n in PER}

        def at(name, h, k):
            return h * PER[name] + k

        block = es.enter_context(nc.Block())

        w_ada_v = w_ada[0].rearrange("(k p) n -> p k n", p=P)
        w_in_v = w_in[0].rearrange("(k p) n -> p k n", p=P)
        w_out_v = w_out[0].rearrange("(k p) n -> p k n", p=P)
        w_gu_v = [ffn_w_in[0, f].rearrange("(k p) (s n) -> p k s n", p=P, s=2) for f in range(2)]
        w_dn_v = [ffn_w_out[0, f].rearrange("(k p) n -> p k n", p=P) for f in range(2)]
        w_qkvz_v = w_in_v[:, :, COL_QKV:COL_BA].rearrange("p k (s n) -> p k s n", s=4)
        NTT = (NTOK // P, SEQ // P, SEQ // P)
        Y_PT = HEADS * DK // P

        def tiles(r, per, t):
            return r * per + (t + 1)

        def loads(r, per, t):
            before = lambda n: 16 * (ADA_TILES // RAW + sum(map(transfers, range(n % RAW, n + 1, RAW))))
            return r * (before(t + per) - before(t)) + before(t)

        def bc(ap, n):
            return ap.unsqueeze(1).broadcast_to([P, n, ap.shape[-1]])

        def mask(i, n=4):
            return bc(mk[:, i, :], n)

        def half(ap, m, d, transposed):
            return ap.rearrange("p n (a r m) -> p (n a) r m", r=2, m=m)[:, :, int((d == 1) != transposed), :]

        def level_mask(d, transposed, lvl):
            return mask(LEVEL + (N_LEVEL if (d == 1) != transposed else 0) + lvl)

        @block.sync
        def _(sp):
            sp.sem_inc(ada_used, RAW)
            sp.sem_inc(ada_evac, 2)
            sp.sem_inc(arow_out[0], 16)
            sp.sem_inc(arow_out[1], 16)
            sp.sem_inc(lo_done, RAW)
            sp.sem_inc(tile_used, HL)
            for i in range(3):
                sp.sem_inc(gated[i], N_OUT * NTT[i])
                sp.sem_inc(added[i], 2)
            sp.sem_inc(HS["y_done"], 1)

            with sp.Fori(0, ADA_N) as nb:
                for j in range(K_TILES):
                    sp.wait_ge(ada_used, nb * K_TILES + (j + 1))
                    sp.dma_start(raw[:, j, :].rearrange("p (k n) -> p k n", k=TILE_K),
                                 w_ada_v[:, TILE_K * j:TILE_K * (j + 1), ds(nb * TILE_N, TILE_N)]
                                 ).then_inc(raw_in[j], 16)
            sp.wait_ge(ada_used, ADA_TILES + RAW)

            def load(r, per, t, src):
                sp.wait_ge(lo_done, tiles(r, per, t))
                dst = raw[:, t % RAW, :].rearrange("p (k n) -> p k n", k=TILE_K)
                if transfers(t) == 1:
                    sp.dma_start(dst, src).then_inc(raw_in[t % RAW], 16)
                else:
                    for a in range(TILE_K):
                        block = dst[:, a]
                        if len(src.shape) == 4:
                            block = block.rearrange("p (s n) -> p s n", s=src.shape[2])
                        sp.dma_start(block, src[:, a]).then_inc(raw_in[t % RAW], 16)

            def ffn_loads(f, base):
                with sp.Fori(0, GROUPS) as g:
                    for j in range(GROUP_TILES):
                        if j < PAIRS * K_TILES:
                            p, k = divmod(j, K_TILES)
                            src = w_gu_v[f][:, TILE_K * k:TILE_K * (k + 1), :,
                                            ds(g * (GROUP_FF * P) + p * 2 * P, 2 * P)]
                        else:
                            n, k = divmod(j - PAIRS * K_TILES, OUT_TILES)
                            src = w_dn_v[f][:, ds(g * GROUP_FF + k * TILE_K, TILE_K),
                                            n * TILE_N:(n + 1) * TILE_N]
                        load(g, GROUP_TILES, base + j, src)

            ffn_loads(0, T_FFN1)
            with sp.Fori(0, HEADS) as h:
                for k in range(K_TILES):
                    load(h, K_TILES, T_HEADS + k,
                         w_qkvz_v[:, TILE_K * k:TILE_K * (k + 1), :, ds(h * DK, DK)])
            with sp.Fori(0, POOL_W // TILE_N) as n:
                for k in range(K_TILES):
                    load(n, K_TILES, T_POOL + k,
                         w_in_v[:, TILE_K * k:TILE_K * (k + 1), ds(n * TILE_N, TILE_N)])
            with sp.Fori(0, N_OUT) as n:
                for k in range(K_TILES):
                    load(n, K_TILES, T_WOUT + k,
                         w_out_v[:, TILE_K * k:TILE_K * (k + 1), ds(n * TILE_N, TILE_N)])
            ffn_loads(1, T_FFN2)
            sp.wait_ge(out_done, 32)

        @block.tensor
        def _(pe):
            mm, turn = nc.tensor.matmul, nc.tensor.transpose

            def product(out, ah, al, bh, bl, first, last):
                mm(out, ah, bh, start=first, stop=False)
                mm(out, ah, bl, start=False, stop=False)
                return mm(out, al, bh, start=False, stop=last)

            def ada():
                pe.wait_ge(id_in, 16)
                pe.wait_ge(c_silu, 1)
                turn(ps[:, 2, 0:32], csil[:], ident[0:32, 0:32]).then_inc(c_turned, 1)
                pe.wait_ge(c_cols, 1)
                with pe.Fori(0, ADA_N // 2) as r:
                    for b in range(2):
                        pe.wait_ge(ada_evac, r * 2 + (b + 1))
                        for j in range(K_TILES):
                            pe.wait_ge(raw_in[j], r * 32 + 16 * (b + 1))
                            for a in range(TILE_K):
                                k = TILE_K * j + a
                                i = mm(ps[0:2, b, :], cT[:, k:32:KT], raw[:, j, a * TILE_N:(a + 1) * TILE_N],
                                       start=(k == 0), stop=(k == KT - 1))
                            i.then_inc(ada_used, 1)
                pe.wait_ge(rows_in, 16 * 9)
                turn(ps[:, 3, 0:128], rows_a[:], ident[:])
                turn(ps[:, 3, 128:208], rows_b[:], ident[0:80, 0:80])
                turn(ps[:, 3, 256:361], rows_c[:], ident[0:105, 0:105]).then_inc(rows_turned, 1)

            def norm(c):
                pe.wait_ge(xn_done, 2 * (c + 1))
                if c == 0:
                    pe.wait_ge(cols_done, 1)
                else:
                    pe.wait_ge(u_done, 4 * c)
                for k in range(KT):
                    for t in range(2):
                        at_ = (k % 2) * SEQ + t * P
                        i = turn(ps[:, k // 2, at_:at_ + P], xn[:, t, k * P:(k + 1) * P], ident[:])
                i.then_inc(x_turned, 1)

            def ffn(f, base, nt):
                with pe.Fori(0, GROUPS) as g:
                    per = N_OUT * NTT[f]
                    for p in range(PAIRS):
                        pe.wait_ge(gated[f], g * per + (3 + p) * NTT[f])
                        for k in range(K_TILES):
                            t = base + p * K_TILES + k
                            pe.wait_ge(lo_done, tiles(g, GROUP_TILES, t) + RAW)
                            for a in range(TILE_K):
                                kk = TILE_K * k + a
                                for q in range(4):
                                    w = slice(a * TILE_N + q * P, a * TILE_N + (q + 1) * P)
                                    i = product(ps[:, 4 * p + q, 0:nt], wh[:, t % HL, w], wl[:, t % HL, w],
                                                xh[:, kk, 0:nt], xl[:, kk, 0:nt], kk == 0, kk == KT - 1)
                            i.then_inc(tile_used, 1)
                    for n in range(N_OUT):
                        if n < 2:
                            pe.wait_ge(F[f]["hf_done"], g * GROUP_FF + 2 * (n + 1))
                        else:
                            pe.wait_ge(gated[f], g * per + (per + (n - 1) * NTT[f]))
                        for k in range(OUT_TILES):
                            t = base + PAIRS * K_TILES + n * OUT_TILES + k
                            if n == 0:
                                pe.wait_ge(F[f]["h_ready"], g * GROUP_FF + TILE_K * (k + 1))
                            pe.wait_ge(lo_done, tiles(g, GROUP_TILES, t) + RAW)
                            for a in range(TILE_K):
                                kk = TILE_K * k + a
                                w = slice(a * TILE_N, (a + 1) * TILE_N)
                                for q in range(NTT[f]):
                                    x_ = slice(q * P, (q + 1) * P)
                                    i = product(ps[:, 4 * (n % 2) + q, :], hth[:, kk, x_], htl[:, kk, x_],
                                                wh[:, t % HL, w], wl[:, t % HL, w],
                                                kk == 0, kk == GROUP_FF - 1)
                            i.then_inc(tile_used, 1)

            def token_tile(r, per, t, k, bank, part=range(TILE_K)):
                if part[0] == 0:
                    pe.wait_ge(lo_done, tiles(r, per, t) + RAW)
                for a in part:
                    kk = TILE_K * k + a
                    w = slice(a * TILE_N, (a + 1) * TILE_N)
                    for q in range(SEQ // P):
                        x_ = slice(q * P, (q + 1) * P)
                        i = product(ps[:, bank + q, :], xh[:, kk, x_], xl[:, kk, x_],
                                    wh[:, t % HL, w], wl[:, t % HL, w], kk == 0, kk == KT - 1)
                if part[-1] == TILE_K - 1:
                    i.then_inc(tile_used, 1)

            def head_tile(h, off, k, part=range(TILE_K)):
                t = T_HEADS + off * K_TILES + k
                if k == 0 and off and part[0] == 0:
                    pe.wait_ge(HS["evac_act"], at("evac_act", h, 2 * off))
                    pe.wait_ge(HS["evac_dve"], at("evac_dve", h, 2 * off))
                if part[0] == 0:
                    pe.wait_ge(lo_done, tiles(h, K_TILES, t) + RAW)
                for a in part:
                    kk = TILE_K * k + a
                    for q, nt in enumerate((SEQ, NTOK, NTOK, SEQ)):
                        w = slice(a * TILE_N + q * P, a * TILE_N + (q + 1) * P)
                        i = product(ps[:, q, 0:nt], wh[:, t % HL, w], wl[:, t % HL, w],
                                    xh[:, kk, 0:nt], xl[:, kk, 0:nt], kk == 0, kk == KT - 1)
                if part[-1] == TILE_K - 1:
                    i.then_inc(tile_used, 1)

            def decay_prep():
                pe.wait_ge(ba_split, 1)
                for q in range(4):
                    for k in range(KT):
                        x_ = slice(q * P, (q + 1) * P)
                        i = product(ps[:, 4, q * N_BA:(q + 1) * N_BA], xh[:, k, x_], xl[:, k, x_],
                                    wbah[:, k, :], wbal[:, k, :], k == 0, k == KT - 1)
                i.then_inc(ba_done, 1)
                pe.wait_ge(prep_dve, PREP_G)
                pe.wait_ge(mk_in, 16)
                for q in range(4):
                    for d in range(2):
                        mm(ps[:, 5, q * 32 + 8 * d:q * 32 + 8 * d + 8], mk[:, CUM + d, :],
                           gp[:, G, q, 8 * d:8 * d + 8], start=True, stop=True)
                    i = mm(ps[:, 5, q * 32 + 16:q * 32 + 32], mk[:, ONES, :], gp[:, G, q, :],
                           start=True, stop=True)
                i.then_inc(prep_pe, 1)

            def gdn(h, block_of):
                def done(i, name):
                    i.then_inc(HS[name], 1)

                def wait(name, k):
                    pe.wait_ge(HS[name], at(name, h, k))

                def fill(*blocks):
                    for b in blocks:
                        block_of(b // TILE_K, b % TILE_K)

                def blk(bank, b):
                    return ps[:, bank, b * P:(b + 1) * P]

                pe.wait_ge(HS["y_done"], at("y_done", h, 1))
                fill(0, 1)
                wait("act_in", 1)
                for q in range(4):
                    i = turn(blk(5, q), kT[:, q // 2, (q % 2) * P:(q % 2 + 1) * P], ident[:])
                done(i, "pe_k")
                fill(2)
                wait("act_in", 2)
                for q in range(4):
                    i = turn(blk(4, q), vT[:, q // 2, (q % 2) * P:(q % 2 + 1) * P], ident[:])
                done(i, "pe_v")
                wait("squared", 2)
                for q in range(6):
                    i = mm(ps[:, 6, q:q + 1], X[:, q, :], mk[:, ONES, 0:1], start=True, stop=True)
                done(i, "pe_ss")
                fill(3, 4)
                wait("kh_set", 1)
                for q in range(4):
                    i = turn(blk(7, q), kh[:, q, :], ident[:])
                done(i, "pe_kh")
                fill(5)
                wait("khT_set", 1)
                for q in range(4):
                    i = mm(blk(5, q), khT[:, q, :], khT[:, q, :], start=True, stop=True)
                done(i, "pe_g")
                wait("hp_set", 1)
                wait("vb_set", 1)
                for d in range(2):
                    for q in range(4):
                        i = mm(blk(4 + 2 * d, q), hp[:, G, q, d:d + 1].broadcast_to([P, P]),
                               mk[:, CUM + d, :], start=True, stop=True)
                    done(i, "pe_cum")
                wait("act_in", 3)
                for q in range(2):
                    i = mm(blk(7, q), qT[:, q * P:(q + 1) * P], khT[:, q, :], start=True, stop=True)
                done(i, "pe_qk")
                fill(6, 7)
                for d in range(2):
                    wait("a_set", d + 1)
                    for q in range(4):
                        i = turn(blk(4 + 2 * d, q), AY[:, 4 * d + q, :], ident[:])
                    done(i, "pe_at")
                wait("aq_set", 1)
                for q in range(4):
                    i = turn(blk(5, q), Aq[:, q, :], ident[:])
                done(i, "pe_aqt")
                fill(8)
                last = len(LEVELS) - 1
                for l in range(last + 1):
                    for d in range(2):
                        wait("lt_set", 2 * l + d + 1)
                        if l == 0:
                            wait("x1_set", d + 1)
                        else:
                            wait("x_set", 2 * (l - 1) + d + 1)
                        for q in range(4):
                            i = mm(blk(4 + 2 * d, q), LE[:, 4 * d + q, :], X[:, 4 * d + q, :],
                                   start=True, stop=True)
                        done(i, "pe_y")
                    for d in range(2):
                        wait("y_set", 2 * l + d + 1)
                        if l == 0:
                            wait("x1_set", 3 + d)
                            wait("aqt_set", 1)
                        else:
                            wait("xt_set", 2 * (l - 1) + d + 1)
                        m = LEVELS[l]

                        def part(bank):
                            return ps[:, bank, q * (P // 2):(q + 1) * (P // 2)].rearrange(
                                "p (a m) -> p a m", m=m)

                        if l < last:
                            for q in range(4):
                                v_ = slice(4 * d + q, 4 * d + q + 1)
                                i = mm(part(4 + 2 * d), XT[:, 4 * d + q, :], half(AY[:, v_, :], m, d, False),
                                       start=True, stop=True)
                            done(i, "pe_z")
                        for q in range(4):
                            v_ = slice(4 * d + q, 4 * d + q + 1)
                            i = mm(part(5 + 2 * d), AY[:, 4 * d + q, :], half(XT[:, v_, :], m, d, True),
                                   start=True, stop=True)
                        done(i, "pe_zt")
                for s in range(4):
                    for d in range(2):
                        q = SCAN[d][s]
                        if s:
                            wait("s_set", 2 * (s - 1) + d + 1)
                            i = mm(blk(4 + 2 * d, 0), khT[:, q, :], S[:, d, :], start=True, stop=True)
                            if s >= 2:
                                if s == 3:
                                    wait("o_set", 3 + d)
                                i = mm(blk(5 + 2 * d, 0), qT[:, q * P:(q + 1) * P], S[:, d, :],
                                       start=True, stop=True)
                            done(i, "pe_r")
                    fill(9 + 2 * s)
                    for d in range(2):
                        q = SCAN[d][s]
                        if s:
                            wait("vbp_set", 2 * (s - 1) + d + 1)
                            rhs = vbp[:, d, :]
                        else:
                            wait("xt_set", 2 * last + d + 1)
                            rhs = vb[:, 4 * d + q, :]
                        i = mm(blk(4 + 2 * d, 1), XT[:, 4 * d + q, :], rhs, start=True, stop=True)
                        done(i, "pe_vn")
                    if s < 3:
                        fill(10 + 2 * s)
                    for d in range(2):
                        q = SCAN[d][s]
                        wait("vn_set", 2 * s + d + 1)
                        if s < 3:
                            if s == 0:
                                wait("kd_set", d + 1)
                            i = mm(blk(4 + 2 * d, 2), LE[:, 4 * d + q, :], vn[:, d, :],
                                   start=True, stop=True)
                            done(i, "pe_kv")
                        if s >= 2:
                            wait("o_set", 4 * (s - 2) + d + 1)
                            i = mm(blk(5 + 2 * d, 1), AqT[:, 2 * d + q, :], vn[:, d, :],
                                   start=True, stop=True)
                            done(i, "pe_av")
                wait("on_set", 1)
                for q in range(2):
                    i = turn(blk(4, q), o[:, q, :], ident[:])
                done(i, "pe_o")

            ada()
            norm(0)
            norm(1)
            pe.wait_ge(x_ready, 8)
            ffn(0, T_FFN1, NTOK)
            norm(2)
            norm(3)
            pe.wait_ge(x_ready, 16)
            for k in range(K_TILES):
                head_tile(0, 0, k)
            decay_prep()
            with pe.Fori(0, HEADS - 1) as h:
                gdn(h, lambda k, a: head_tile(h, 1, k, (a,)))
            pe.wait_ge(HS["evac_act"], 2 * HEADS)
            pe.wait_ge(HS["evac_dve"], 2 * HEADS)
            gdn(HEADS - 1, lambda k, a: token_tile(0, 0, T_POOL + k, k, 0, (a,)))
            for k in range(K_TILES):
                token_tile(0, 0, T_POOL + K_TILES + k, k, 2)
            pe.wait_ge(pool_u, 4)
            pe.wait_ge(pool_in, 16 * 3)
            pe.wait_ge(HS["y_done"], 1 + HEADS)
            for c_ in range(8):
                for q in range(2):
                    i = mm(ps[:, 4 + c_ // 2, (c_ % 2) * SEQ:(c_ % 2 + 1) * SEQ],
                           u[:, q, c_ * P:(c_ + 1) * P], pg[:, q, c_ // 2, :],
                           start=(q == 0), stop=(q == 1))
            i.then_inc(pool_pe, 1)
            pe.wait_ge(pool_p, 4)
            for c_ in range(8):
                for q in range(2):
                    i = mm(ps[:, c_ // 2, (c_ % 2) * SEQ:(c_ % 2 + 1) * SEQ],
                           wp[:, c_ // 2, q, (c_ % 2) * P:(c_ % 2 + 1) * P],
                           pT[:, c_ // 2 * 2 + q, :], start=(q == 0), stop=(q == 1))
            i.then_inc(pool_pe2, 1)
            pe.wait_ge(y_ready, 2)
            with pe.Fori(0, N_OUT // 2) as r:
                for n in range(2):
                    pe.wait_ge(gated[2], r * (2 * NTT[2]) + (n + 1) * NTT[2] + 2 * NTT[2])
                    for k in range(K_TILES):
                        token_tile(r, 2 * K_TILES, T_WOUT + n * K_TILES + k, k, 4 * n)
            norm(4)
            pe.wait_ge(x_ready, 20)
            ffn(1, T_FFN2, SEQ)

        @block.scalar
        def _(act):
            fn = nc.scalar.activation

            def split(r, per, t):
                if t >= T_END:
                    return
                act.wait_ge(raw_in[t % RAW], loads(r, per, t))
                act.wait_ge(tile_used, tiles(r, per, t))
                nc.scalar.copy(wh[:, t % HL, :], raw[:, t % RAW, :]).then_inc(hi_done, 1)

            def start():
                act.dma_start(ident[:], ident_in).then_inc(id_in, 16)
                act.dma_start(crow[0:16, :], c.rearrange("b (k p) -> (b k) p", p=P)).then_inc(c_in, 16)
                act.dma_start(crow[16:32, :], c_ctx.rearrange("(k p) -> k p", p=P)).then_inc(c_in, 16)
                act.dma_start(h_lat[:], x[0].rearrange("(t p) n -> p t n", p=P)).then_inc(x_in, 16)
                act.dma_start(h_ctx[:], ctx[0].rearrange("(t p) n -> p t n", p=P)).then_inc(x_in, 16)
                act.dma_start(gates[:], pos.rearrange("(t p) n -> p t n", p=P)).then_inc(x_in, 16)
                act.dma_start(rows_b[32:80, :], norm_g[0].rearrange("n (k p) -> (n k) p", p=P)).then_inc(rows_in, 16)
                act.dma_start(rows_c[0:96, :], conv_w[0].rearrange("j (r p) -> (j r) p", p=P)).then_inc(rows_in, 16)
                act.dma_start(rows_c[96:104, :], pool_scale[0].rearrange("(k p) -> k p", p=P)).then_inc(rows_in, 16)
                act.dma_start(rows_c[104:105, :], o_norm_g).then_inc(rows_in, 16)
                act.wait_ge(c_in, 32)
                fn(csil[:], crow[:], ACT.Silu).then_inc(c_silu, 1)

            def ada():
                with act.Fori(0, ADA_N // 2) as r:
                    for b in range(2):
                        act.wait_ge(ada_evac, r * 2 + (b + 1))
                        act.dma_start(brow[:, b, :], b_ada[0:1, ds(r * (2 * TILE_N) + b * TILE_N, TILE_N)]
                                      .broadcast_to([2, TILE_N])).then_inc(brow_in[b], 16)
                    for b in range(2):
                        act.wait_ge(ada_evac, r * 2 + (b + 3))
                        act.dma_start(ada_rows[:, ds(r * (2 * TILE_N) + b * TILE_N, TILE_N)],
                                      arow[:, b, :]).then_inc(arow_out[b], 16)
                for b in range(2):
                    act.wait_ge(arow_out[b], 16 * (1 + ADA_N // 2))
                rows = ada_rows.rearrange("s (k p) -> s k p", p=P)
                for s in range(2):
                    for m in range(2):
                        act.dma_start(rows_a[64 * s + 32 * m:64 * s + 32 * m + 32, :],
                                      rows[s, 48 * m:48 * m + 32, :]).then_inc(rows_in, 16)
                act.dma_start(rows_b[0:32, :], rows[0, 96:128, :]).then_inc(rows_in, 16)
                act.wait_ge(h_set, 1)
                for s in range(2):
                    act.dma_start(gates[:, s, :], ada_rows[s:s + 1, 2 * D:3 * D].broadcast_to([P, D])
                                  ).then_inc(gates_in, 16)

            def mean_squares(c_, src):
                for t in range(2):
                    fn(xn[:, t, :], src[:, t, :], ACT.Square, accum_out=n_ss[:, t:t + 1]).then_inc(ss_done, 1)

            def norm(c_, src):
                if c_ % 2:
                    act.wait_ge(x_ready, 4 * c_)
                mean_squares(c_, src)
                act.wait_ge(rstd_done, c_ + 1)
                fn(xn[:, 0, :], src[:, 0, :], ACT.Copy, scale=n_rstd[:, 0:1]).then_inc(xn_done, 1)
                act.wait_ge(x_turned, c_ + 1)
                shift = (cols_a[:, 0:16], cols_a[:, 64:80], cols_a[:, 32:48], cols_a[:, 96:112],
                         cols_b[:, 0:16])[c_]
                for k in range(KT):
                    i = fn(uk[:, k, :], ps[:, k // 2, (k % 2) * SEQ:(k % 2 + 1) * SEQ], ACT.Identity,
                           bias=shift[:, k:k + 1], scale=scale_c[:, c_, k:k + 1])
                    if k % 4 == 3:
                        i.then_inc(u_done, 1)

            def hidden(f, g, base, p, nt):
                s = F[f]
                act.wait_ge(tile_used, tiles(g, GROUP_TILES, base + (p + 1) * K_TILES - 1) + HL)
                for b in range(2):
                    fn(sg[:, b, 0:nt], ps[:, 4 * p + b, 0:nt], ACT.Silu).then_inc(s["silu_done"], 1)
                for b in range(2):
                    act.wait_ge(s["hf_done"], g * GROUP_FF + (2 * p + b + 1))
                    nc.scalar.copy(hth[:, 2 * p + b, 0:nt], hf[:, b, 0:nt]).then_inc(s["hh_done"], 1)

            def ffn(f, base, nt):
                def group(g, per):
                    for j in range(GROUP_TILES):
                        split(g, per, base + j + AHEAD)
                        if j in (K_TILES - 1, 2 * K_TILES - 1):
                            hidden(f, g, base, j // K_TILES, nt)
                if base + GROUPS * GROUP_TILES < T_END:
                    with act.Fori(0, GROUPS) as g:
                        group(g, GROUP_TILES)
                else:
                    with act.Fori(0, GROUPS - 1) as g:
                        group(g, GROUP_TILES)
                    g = GROUPS - 1
                    for j in range(GROUP_TILES):
                        split(0, 0, base + g * GROUP_TILES + j + AHEAD)
                        if j in (K_TILES - 1, 2 * K_TILES - 1):
                            hidden(f, g, base, j // K_TILES, nt)

            def head_out(h, off):
                act.wait_ge(tile_used, tiles(h, K_TILES, T_HEADS + (off + 1) * K_TILES - 1) + HL)
                for b, dst in ((1, pk), (2, pv)):
                    nc.scalar.copy(dst[:, :, CONV_LEFT:CONV_LEFT + SEQ],
                                   ps[:, b, :].rearrange("p (s n) -> p s n", s=2)).then_inc(HS["evac_act"], 1)

            def decay_prep():
                act.wait_ge(prep_dve, 1)
                ba = ps[:, 4, 0:4 * N_BA].rearrange("p (t n) -> p t n", t=4)
                fn(gp[:, BETA], ba[:, :, 0:16], ACT.Sigmoid).then_inc(prep_act, 1)
                fn(rowc[:, 1, :], rowc[:, 1, :], ACT.Exp).then_inc(prep_act, 1)
                act.wait_ge(prep_dve, 2)
                fn(sp_t[:, 1], sp_t[:, 1], ACT.Exp, scale=-1.0).then_inc(prep_act, 1)
                act.wait_ge(prep_pe, 1)
                sums = ps[:, 5, 0:128].rearrange("p (t n) -> p t n", t=4)
                fn(gp[:, EG], sums[:, :, 0:16], ACT.Exp).then_inc(prep_act, 1)
                fn(gp[:, EGT], sums[:, :, 16:32], ACT.Exp).then_inc(prep_act, 1)
                act.wait_ge(prep_dve, PREP_G + 2)
                fn(gp[:, EKD], gp[:, EKD], ACT.Exp).then_inc(prep_act, 1)

            def gdn(h, point, tail):
                def done(i, name):
                    i.then_inc(HS[name], 1)

                def wait(name, k):
                    act.wait_ge(HS[name], at(name, h, k))

                def quad(bank):
                    return ps[:, bank, :].rearrange("p (q n) -> p q n", q=4)

                point(0)
                wait("conv", CONV_W)
                done(fn(kT[:], kT[:], ACT.Silu), "act_in")
                wait("act_in", 1)
                done(fn(X[:, 0:4, :].rearrange("p a b -> p (a b)"), kT[:].rearrange("p a b -> p (a b)"), ACT.Square), "squared")
                wait("conv", 2 * CONV_W)
                done(fn(vT[:], vT[:], ACT.Silu), "act_in")
                wait("conv", 3 * CONV_W)
                done(fn(qT[:], qT[:], ACT.Silu), "act_in")
                wait("act_in", 3)
                done(fn(X[:, 4:6, :].rearrange("p a b -> p (a b)"), qT[:], ACT.Square), "squared")
                wait("evac_dve", 2)
                done(fn(zs[:], pz[:], ACT.Silu), "act_in")
                point(1)
                wait("pe_v", 1)
                wait("hp_set", 1)
                for v_ in range(8):
                    i = fn(vb[:, v_, :], ps[:, 4, (v_ % 4) * P:(v_ % 4 + 1) * P], ACT.Copy,
                           scale=hp[:, BETA, v_ % 4, v_ // 4:v_ // 4 + 1])
                done(i, "vb_set")
                point(2)
                wait("pe_kh", 1)
                done(nc.scalar.copy(khT[:], quad(7)), "khT_set")
                point(3)
                for d in range(2):
                    wait("dd_set", d + 1)
                    done(fn(LE[:, 4 * d:4 * d + 4, :], LE[:, 4 * d:4 * d + 4, :], ACT.Exp, scale=-1.0), "e_set")
                for d in range(2):
                    wait("pe_at", d + 1)
                    done(nc.scalar.copy(AT[:, 4 * d:4 * d + 4, :], quad(4 + 2 * d)), "at_set")
                wait("pe_aqt", 1)
                done(nc.scalar.copy(AqT[:], quad(5)), "aqt_set")
                point(4)
                for l in range(len(LEVELS)):
                    for d in range(2):
                        wait("pe_y", 2 * l + d + 1)
                        done(nc.scalar.copy(AY[:, 4 * d:4 * d + 4, :], quad(4 + 2 * d)), "y_set")
                for s in range(4):
                    for d in range(2):
                        wait("pe_vn", 2 * s + d + 1)
                        done(nc.scalar.copy(vn[:, d, :], ps[:, 4 + 2 * d, P:2 * P]), "vn_set")
                    if s < 3:
                        point(5 + s)
                tail()
                wait("osc", 1)
                for q in range(2):
                    i = fn(vbp[:, q, :], o[:, q, :], ACT.Square, accum_out=oss[:, q:q + 1])
                done(i, "oss_set")

            start()
            ada()
            act.wait_ge(scale_done, 5)
            act.wait_ge(h_set, 1)
            for t in range(AHEAD):
                split(0, 0, t)
            norm(0, h_lat)
            norm(1, h_ctx)
            ffn(0, T_FFN1, NTOK)
            act.wait_ge(added[0], GROUPS * N_OUT * NTT[0] + 2)
            norm(2, h_lat)
            norm(3, h_ctx)
            act.wait_ge(x_ready, 16)
            act.dma_start(wba[:], w_in_v[:, :, COL_BA:COL_BA + N_BA]).then_inc(ba_in, 16)
            act.dma_start(rowc[:, 0, :], dt_bias.rearrange("l d h -> l (d h)").broadcast_to([P, 16])).then_inc(rowc_in, 16)
            act.dma_start(rowc[:, 1, :], a_log.rearrange("l d h -> l (d h)").broadcast_to([P, 16])).then_inc(rowc_in, 16)
            act.dma_start(mk[:], masks_in.rearrange("p (m n) -> p m n", n=P)).then_inc(mk_in, 16)
            for k in range(K_TILES):
                split(0, 0, T_HEADS + k + AHEAD)
            act.wait_ge(ba_in, 16)
            nc.scalar.copy(wbah[:], wba[:]).then_inc(ba_hi, 1)
            head_out(0, 0)
            decay_prep()
            with act.Fori(0, HEADS - 1) as h:
                gdn(h, lambda k: split(h, K_TILES, T_HEADS + K_TILES + k + AHEAD), lambda: head_out(h, 1))
            gdn(HEADS - 1, lambda k: split(0, 0, T_POOL + k + AHEAD), lambda: None)
            act.wait_ge(HS["y_done"], HEADS + 1)
            act.dma_start(pg[:], pools_in.rearrange("(t p) (g n) -> p t g n", p=P, g=4)).then_inc(pool_in, 16)
            for s in range(2):
                act.dma_start(wp[:, 2 * s:2 * s + 2], w_pool[0, 2 * s:2 * s + 2].rearrange("g (t p) n -> p g t n", p=P)
                              ).then_inc(pool_in, 16)
            for q in range(2):
                nc.scalar.copy(u[:, q, 0:TILE_N], ps[:, q, :]).then_inc(pool_u, 1)
            for k in range(K_TILES):
                split(0, 0, T_POOL + K_TILES + k + AHEAD)
            act.wait_ge(tile_used, T_WOUT + HL)
            for q in range(2):
                nc.scalar.copy(u[:, q, TILE_N:2 * TILE_N], ps[:, 2 + q, :]).then_inc(pool_u, 1)
            act.wait_ge(pool_pe, 1)
            for b in range(2):
                nc.scalar.copy(pT[:, 2 * b:2 * b + 2, :].rearrange("p a b -> p (a b)"), ps[:, 4 + b, :]
                               ).then_inc(pool_p, 1)
            act.wait_ge(pool_pe2, 1)
            for c_ in range(8):
                i = fn(yp[:, c_, :], ps[:, c_ // 2, (c_ % 2) * SEQ:(c_ % 2 + 1) * SEQ], ACT.Copy,
                       scale=cols_c[:, 96 + c_:97 + c_])
            i.then_inc(yp_done, 1)
            act.wait_ge(y_ready, 2)
            for s in range(2):
                act.dma_start(gates[:, s, :], ada_rows[0:1, (5 + 3 * s) * D:(6 + 3 * s) * D].broadcast_to([P, D])
                              ).then_inc(gates_in2, 16)
            for k in range(N_OUT * K_TILES):
                split(0, 0, T_WOUT + k + AHEAD)
            act.wait_ge(added[2], N_OUT * NTT[2] + 2)
            act.dma_start(gates[:, 0, :], final_g.unsqueeze(0).broadcast_to([P, D])).then_inc(fg_in, 16)
            norm(4, h_lat)
            ffn(1, T_FFN2, SEQ)
            act.wait_ge(added[1], GROUPS * N_OUT * NTT[1] + 2)
            mean_squares(5, h_lat)
            for t in range(2):
                act.wait_ge(xn_done, 10 + t + 1)
                act.dma_start(out[0].rearrange("(t p) n -> p t n", p=P)[:, t, :], xn[:, t, :]).then_inc(out_done, 16)

        @block.vector
        def _(dve):
            V = nc.vector
            tt, ts, stt = V.tensor_tensor, V.tensor_scalar, V.scalar_tensor_tensor

            def split(r, per, t):
                if t >= T_END:
                    return
                dve.wait_ge(hi_done, tiles(r, per, t))
                tt(wl[:, t % HL, :], raw[:, t % RAW, :], wh[:, t % HL, :].bitcast(F32), ALU.subtract
                   ).then_inc(lo_done, 1)

            def ada():
                dve.wait_ge(c_turned, 1)
                V.tensor_copy(cT[:], ps[:, 2, 0:32]).then_inc(c_cols, 1)
                dve.wait_ge(x_in, 48)
                tt(h_lat[:], h_lat[:], gates[:], ALU.add).then_inc(h_set, 1)
                with dve.Fori(0, ADA_N // 2) as r:
                    for b in range(2):
                        dve.wait_ge(ada_used, r * (2 * K_TILES) + ((b + 1) * K_TILES + RAW))
                        dve.wait_ge(brow_in[b], r * 16 + 16)
                        dve.wait_ge(arow_out[b], r * 16 + 16)
                        tt(arow[:, b, :], ps[0:2, b, :], brow[:, b, :], ALU.add).then_inc(ada_evac, 1)
                dve.wait_ge(rows_turned, 1)
                V.tensor_copy(cols_a[:], ps[:, 3, 0:128])
                V.tensor_copy(cols_b[:], ps[:, 3, 128:208])
                V.tensor_copy(cols_c[:], ps[:, 3, 256:361]).then_inc(cols_done, 1)
                dve.wait_ge(cols_done, 1)
                for i, (sc_, n) in enumerate(((cols_a[:, 16:32], 0), (cols_a[:, 80:96], 0), (cols_a[:, 48:64], 1),
                                              (cols_a[:, 112:128], 1), (cols_b[:, 16:32], 2))):
                    stt(scale_c[:, i, :], sc_, 1.0, cols_b[:, 32 + 16 * n:48 + 16 * n], ALU.add, ALU.mult
                        ).then_inc(scale_done, 1)

            def rstd(c_):
                dve.wait_ge(ss_done, 2 * (c_ + 1))
                ts(n_ms[:], n_ss[:], 1.0 / D, EPS, ALU.mult, ALU.add).then_inc(ms_done, 1)
                dve.wait_ge(rstd_done, c_ + 1)

            def norm(c_, src):
                rstd(c_)
                ts(xn[:, 1, :], src[:, 1, :], n_rstd[:, 1:2], None, ALU.mult).then_inc(xn_done, 1)
                s = slice(SEQ, NTOK) if c_ in (1, 3) else slice(0, SEQ)
                for b in range(4):
                    k = slice(4 * b, 4 * b + 4)
                    dve.wait_ge(u_done, 4 * c_ + b + 1)
                    V.tensor_copy(xh[:, k, s], uk[:, k, :]).then_inc(uh_done, 1)
                    dve.wait_ge(uh_done, 4 * c_ + b + 1)
                    tt(xl[:, k, s], uk[:, k, :], xh[:, k, s].bitcast(F32), ALU.subtract).then_inc(x_ready, 1)

            def gate_out(ph, r, per_r, first, used, bank, n, factor, gate_of):
                dve.wait_ge(tile_used, used)
                for q in range(NTT[ph]):
                    idx = first + q
                    dve.wait_ge(added[ph], r * per_r + (idx + 1))
                    stt(tmp[:, idx % 2, :], ps[:, bank + q, :], factor,
                        gates[:, gate_of(q), n * TILE_N:(n + 1) * TILE_N], ALU.mult, ALU.mult
                        ).then_inc(gated[ph], 1)

            def ffn(f, base, nt):
                s = F[f]
                dve.wait_ge(gates_in if f == 0 else gates_in2, 32)
                gate_of = (lambda q: q // 2) if f == 0 else (lambda q: 1)

                def hidden(g, p):
                    for b in range(2):
                        dve.wait_ge(s["silu_done"], g * GROUP_FF + (2 * p + b + 1))
                        tt(hf[:, b, 0:nt], sg[:, b, 0:nt], ps[:, 4 * p + 2 + b, 0:nt], ALU.mult
                           ).then_inc(s["hf_done"], 1)
                    for b in range(2):
                        dve.wait_ge(s["hh_done"], g * GROUP_FF + (2 * p + b + 1))
                        tt(htl[:, 2 * p + b, 0:nt], hf[:, b, 0:nt], hth[:, 2 * p + b, 0:nt].bitcast(F32),
                           ALU.subtract).then_inc(s["h_ready"], 1)

                def group(r, per, g, t0):
                    for j in range(GROUP_TILES):
                        split(r, per, t0 + j + AHEAD)
                        if j in (K_TILES - 1, 2 * K_TILES - 1):
                            hidden(g, j // K_TILES)
                        elif j >= PAIRS * K_TILES and j % OUT_TILES == OUT_TILES - 1:
                            n = (j - PAIRS * K_TILES) // OUT_TILES
                            gate_out(f, g, N_OUT * NTT[f], n * NTT[f], tiles(r, per, t0 + j) + HL,
                                     4 * (n % 2), n, 0.5, gate_of)

                whole = GROUPS if f == 0 else GROUPS - 1
                with dve.Fori(0, whole) as g:
                    group(g, GROUP_TILES, g, base)
                if whole < GROUPS:
                    group(0, 0, whole, base + whole * GROUP_TILES)

            def head_out(h, off):
                dve.wait_ge(tile_used, tiles(h, K_TILES, T_HEADS + (off + 1) * K_TILES - 1) + HL)
                V.tensor_copy(pq[:, CONV_LEFT:CONV_LEFT + SEQ], ps[:, 0, 0:SEQ]).then_inc(HS["evac_dve"], 1)
                if off:
                    dve.wait_ge(HS["act_in"], at("act_in", h, 4))
                V.tensor_copy(pz[:], ps[:, 3, 0:SEQ]).then_inc(HS["evac_dve"], 1)

            def decay_prep():
                n = [0]

                def link(i):
                    n[0] += 1
                    i.then_inc(prep_dve, 1)
                    dve.wait_ge(prep_dve, n[0])

                ba = ps[:, 4, 0:4 * N_BA].rearrange("p (t n) -> p t n", t=4)
                xg, e, r_, s2, q_, m = (sp_t[:, i] for i in range(6))
                dve.wait_ge(ba_done, 1)
                dve.wait_ge(rowc_in, 32)
                link(tt(xg, ba[:, :, 16:32], bc(rowc[:, 0, :], 4), ALU.add))
                link(stt(e, xg, -1.0, xg, ALU.mult, ALU.max))
                dve.wait_ge(prep_act, 3)
                link(ts(r_, e, 2.0, None, ALU.add))
                link(V.reciprocal(r_, r_))
                link(tt(e, e, r_, ALU.mult))
                link(tt(s2, e, e, ALU.mult))
                link(ts(q_, s2, 1.0 / 15, None, ALU.mult))
                for o_ in (13, 11, 9, 7, 5, 3):
                    link(stt(q_, q_, 1.0 / o_, s2, ALU.add, ALU.mult))
                link(stt(q_, q_, 1.0, e, ALU.add, ALU.mult))
                link(ts(m, xg, 0.0, None, ALU.max))
                link(stt(q_, q_, 2.0, m, ALU.mult, ALU.add))
                link(stt(gp[:, G], q_, -1.0, bc(rowc[:, 1, :], 4), ALU.mult, ALU.mult))
                assert n[0] == PREP_G
                dve.wait_ge(prep_pe, 1)
                dve.wait_ge(prep_act, 5)
                sums = ps[:, 5, 0:128].rearrange("p (t n) -> p t n", t=4)
                link(V.tensor_copy(gp[:, GC], sums[:, :, 0:16]))
                link(tt(gp[:, EKD], sums[:, :, 16:32], gp[:, GC], ALU.subtract))
                dve.wait_ge(prep_act, 4)
                link(stt(gp[:, NBEG], gp[:, BETA], -1.0, gp[:, EG], ALU.mult, ALU.mult))
                dve.wait_ge(prep_act, 6)

            def gdn(h, point, tail):
                def done(i, name):
                    i.then_inc(HS[name], 1)

                def wait(name, k):
                    dve.wait_ge(HS[name], at(name, h, k))

                def quad(bank):
                    return ps[:, bank, :].rearrange("p (q n) -> p q n", q=4)

                done(V.tensor_copy(hp[:].rearrange("p k t d -> p (k t) d"),
                                   gp[:].rearrange("p k t (d h) -> p (k t) d h", h=HEADS)[:, :, :, h]
                                   if isinstance(h, int) else
                                   gp[:].rearrange("p k t (d h) -> p (k t) d h", h=HEADS)[:, :, :, ds(h, 1)]
                                   .rearrange("p a d o -> p a (d o)")), "hp_set")
                taps = cols_c[:, 0:96].rearrange("p (a h) -> p a h", h=HEADS)
                done(V.tensor_copy(cw[:].unsqueeze(2), taps[:, :, ds(h, 1)]), "cw_set")
                point(0)
                wait("cw_set", 1)
                wait("evac_act", 2)
                wait("evac_dve", 2)
                for n, (buf, dst, c_) in enumerate(((pk, kT, 1), (pv, vT, 2), (pq, qT, 0))):
                    for j in range(CONV_W):
                        tap = cw[:, 3 * j + c_:3 * j + c_ + 1]
                        src = buf[:, j:j + SEQ] if buf is pq else buf[:, :, j:j + SEQ]
                        if j == 0:
                            i = ts(dst[:], src, tap, None, ALU.mult)
                        else:
                            wait("conv", CONV_W * n + j)
                            i = stt(dst[:], src, tap, dst[:], ALU.mult, ALU.add)
                        done(i, "conv")
                point(1)
                wait("pe_ss", 1)
                done(ts(ssb[:], ps[:, 6, 0:6], EPS, None, ALU.add), "ss_sb")
                wait("rs_set", 1)
                wait("pe_k", 1)
                for q in range(4):
                    i = ts(kh[:, q, :], ps[:, 5, q * P:(q + 1) * P], rs[:, q:q + 1], None, ALU.mult)
                done(i, "kh_set")
                done(ts(rq[:], rs[:, 4:6], DK ** -0.5, None, ALU.mult), "rq_set")
                point(2)
                for d in range(2):
                    wait("pe_cum", d + 1)
                    for q in range(4):
                        i = stt(LE[:, 4 * d + q, :], ps[:, 4 + 2 * d, q * P:(q + 1) * P],
                                hp[:, GC, q, d:d + 1], mk[:, MASKED + d, :], ALU.subtract, ALU.max)
                    done(i, "dd_set")
                wait("pe_g", 1)
                for d in range(2):
                    wait("e_set", d + 1)
                    for q in range(4):
                        i = stt(AY[:, 4 * d + q, :], LE[:, 4 * d + q, :], hp[:, BETA, q, d:d + 1],
                                ps[:, 5, q * P:(q + 1) * P], ALU.mult, ALU.mult)
                    done(i, "a_set")
                wait("ei_set", 1)
                wait("pe_qk", 1)
                for d in range(2):
                    i = tt(Aq[:, 2 * d:2 * d + 2, :], Aq[:, 2 * d:2 * d + 2, :],
                           ps[:, 7, 0:2 * P].rearrange("p (q n) -> p q n", q=2), ALU.mult)
                done(i, "aq_set")
                point(3)
                for k, buf in enumerate((X, X, XT, XT)):
                    d = k % 2
                    b = slice(4 * d, 4 * d + 4)
                    if k < 2:
                        wait("m1_set", d + 1)
                    else:
                        wait("at_set", d + 1)
                        done(tt(XT[:, b, :], AT[:, b, :], level_mask(d, True, 0), ALU.mult), "mt_set")
                        wait("mt_set", d + 1)
                    done(tt(buf[:, b, :], bc(ident[:], 4), buf[:, b, :], ALU.subtract), "x1_set")
                point(4)
                last = len(LEVELS) - 1
                for l in range(last + 1):
                    for d in range(2):
                        b = slice(4 * d, 4 * d + 4)
                        m = LEVELS[l]
                        if l < last:
                            wait("pe_z", 2 * l + d + 1)
                            part = half(X[:, b, :], m, d, False)
                            done(tt(part, part, ps[:, 4 + 2 * d, 0:SEQ].rearrange("p (a m) -> p a m", m=m),
                                    ALU.subtract), "x_set")
                        wait("pe_zt", 2 * l + d + 1)
                        part = half(XT[:, b, :], m, d, True)
                        done(tt(part, part, ps[:, 5 + 2 * d, 0:SEQ].rearrange("p (a m) -> p a m", m=m),
                                ALU.subtract), "xt_set")
                wait("vb_set", 1)
                for s in range(4):
                    for d in range(2):
                        q = SCAN[d][s]
                        if s:
                            wait("pe_r", 2 * (s - 1) + d + 1)
                            done(stt(vbp[:, d, :], ps[:, 4 + 2 * d, 0:P], hp[:, NBEG, q, d:d + 1],
                                     vb[:, 4 * d + q, :], ALU.mult, ALU.add), "vbp_set")
                        if s == 2:
                            done(ts(o[:, q, :], ps[:, 5 + 2 * d, 0:P], hp[:, EG, q, d:d + 1], None,
                                    ALU.mult), "o_set")
                        if s == 3:
                            wait("o_set", 4)
                            done(stt(o[:, q, :], ps[:, 5 + 2 * d, 0:P], hp[:, EG, q, d:d + 1],
                                     o[:, q, :], ALU.mult, ALU.add), "o_set")
                    for d in range(2):
                        q = SCAN[d][s]
                        if s < 3:
                            wait("pe_kv", 2 * s + d + 1)
                            if s == 0:
                                i = V.tensor_copy(S[:, d, :], ps[:, 4 + 2 * d, 2 * P:3 * P])
                            else:
                                i = stt(S[:, d, :], S[:, d, :], hp[:, EGT, q, d:d + 1],
                                        ps[:, 4 + 2 * d, 2 * P:3 * P], ALU.mult, ALU.add)
                            done(i, "s_set")
                        if s >= 2:
                            wait("pe_av", 2 * (s - 2) + d + 1)
                            wait("o_set", 4 * (s - 2) + d + 1 if s == 2 else 6)
                            done(tt(o[:, q, :], o[:, q, :], ps[:, 5 + 2 * d, P:2 * P], ALU.add), "o_set")
                    if s < 3:
                        point(5 + s)
                tail()
                wait("o_set", 8)
                for q in range(2):
                    i = ts(o[:, q, :], o[:, q, :], rq[:, q:q + 1], None, ALU.mult)
                done(i, "osc")
                wait("oss_set", 1)
                done(ts(oms[:], oss[:], 1.0 / DK, EPS, ALU.mult, ALU.add), "oms_set")
                wait("ors_set", 1)
                for q in range(2):
                    i = ts(o[:, q, :], o[:, q, :], ors[:, q:q + 1], None, ALU.mult)
                done(i, "on_set")
                wait("pe_o", 1)
                wait("act_in", 4)
                done(stt(yg[:, ds(h, 1), :], ps[:, 4:5, 0:SEQ], cols_c[:, 104:105], zs[:].unsqueeze(1),
                         ALU.mult, ALU.mult), "y_done")

            ada()
            for t in range(AHEAD):
                split(0, 0, t)
            norm(0, h_lat)
            norm(1, h_ctx)
            ffn(0, T_FFN1, NTOK)
            dve.wait_ge(added[0], GROUPS * N_OUT * NTT[0] + 2)
            norm(2, h_lat)
            norm(3, h_ctx)
            for b_ in (pq[:, 0:CONV_LEFT], pq[:, CONV_LEFT + SEQ:], pk[:, :, 0:CONV_LEFT],
                       pk[:, :, CONV_LEFT + SEQ:], pv[:, :, 0:CONV_LEFT], pv[:, :, CONV_LEFT + SEQ:]):
                i = V.memset(b_, 0.0)
            i.then_inc(margins_set, 1)
            dve.wait_ge(margins_set, 1)
            for k in range(K_TILES):
                split(0, 0, T_HEADS + k + AHEAD)
            dve.wait_ge(ba_hi, 1)
            tt(wbal[:], wba[:], wbah[:].bitcast(F32), ALU.subtract).then_inc(ba_split, 1)
            head_out(0, 0)
            decay_prep()
            with dve.Fori(0, HEADS - 1) as h:
                gdn(h, lambda k: split(h, K_TILES, T_HEADS + K_TILES + k + AHEAD), lambda: head_out(h, 1))
            gdn(HEADS - 1, lambda k: split(0, 0, T_POOL + k + AHEAD), lambda: None)
            for k in range(K_TILES):
                split(0, 0, T_POOL + K_TILES + k + AHEAD)
            dve.wait_ge(pool_pe, 1)
            for b in range(2, 4):
                V.tensor_copy(pT[:, 2 * b:2 * b + 2, :].rearrange("p a b -> p (a b)"), ps[:, 4 + b, :]
                              ).then_inc(pool_p, 1)
            dve.wait_ge(HS["y_done"], HEADS + 1)
            V.tensor_copy(xh[:, 8:16, 0:SEQ], yg[:]).then_inc(y_hi, 1)
            dve.wait_ge(y_hi, 1)
            tt(xl[:, 8:16, 0:SEQ], yg[:], xh[:, 8:16, 0:SEQ].bitcast(F32), ALU.subtract).then_inc(y_ready, 1)
            dve.wait_ge(yp_done, 1)
            V.tensor_copy(xh[:, 0:8, 0:SEQ], yp[:]).then_inc(y_hi, 1)
            dve.wait_ge(y_hi, 2)
            tt(xl[:, 0:8, 0:SEQ], yp[:], xh[:, 0:8, 0:SEQ].bitcast(F32), ALU.subtract).then_inc(y_ready, 1)
            dve.wait_ge(gates_in2, 32)
            for n in range(N_OUT):
                for k in range(K_TILES):
                    split(0, 0, T_WOUT + n * K_TILES + k + AHEAD)
                gate_out(2, 0, 0, n * NTT[2], T_WOUT + (n + 1) * K_TILES + HL, 4 * (n % 2), n, 1.0, lambda q: 0)
            dve.wait_ge(added[2], N_OUT * NTT[2] + 2)
            norm(4, h_lat)
            ffn(1, T_FFN2, SEQ)
            dve.wait_ge(fg_in, 16)
            dve.wait_ge(added[1], GROUPS * N_OUT * NTT[1] + 2)
            rstd(5)
            for t in range(2):
                stt(xn[:, t, :], h_lat[:, t, :], n_rstd[:, t:t + 1], gates[:, 0, :], ALU.mult, ALU.mult
                    ).then_inc(xn_done, 1)

        @block.gpsimd
        def _(pool):
            tt = nc.gpsimd.tensor_tensor

            def rstd(c_):
                pool.wait_ge(ms_done, c_ + 1)
                tt(n_rstd[:], n_ms[:], mhalf[:, 0:2], ALU.pow).then_inc(rstd_done, 1)

            def add_out(ph, groups, where):
                per = N_OUT * NTT[ph]

                def blocks(g):
                    for n in range(N_OUT):
                        for q in range(NTT[ph]):
                            idx = n * NTT[ph] + q
                            pool.wait_ge(gated[ph], g * per + (idx + 1 + per))
                            dst = where[q // 2][:, q % 2, n * TILE_N:(n + 1) * TILE_N]
                            tt(dst, dst, tmp[:, idx % 2, :], ALU.add).then_inc(added[ph], 1)
                if groups == 1:
                    blocks(0)
                else:
                    with pool.Fori(0, groups) as g:
                        blocks(g)

            def gdn(h):
                def done(i, name):
                    i.then_inc(HS[name], 1)

                def wait(name, k):
                    pool.wait_ge(HS[name], at(name, h, k))

                wait("ss_sb", 1)
                done(tt(rs[:], ssb[:], mhalf[:, 0:6], ALU.pow), "rs_set")
                for d in range(2):
                    wait("e_set", d + 1)
                    i = tt(Aq[:, 2 * d:2 * d + 2, :], LE[:, 4 * d:4 * d + 2, :], bc(ident[:], 2), ALU.add)
                done(i, "ei_set")
                for d in range(2):
                    b = slice(4 * d, 4 * d + 4)
                    wait("a_set", d + 1)
                    done(tt(X[:, b, :], AY[:, b, :], level_mask(d, False, 0), ALU.mult), "m1_set")
                wait("ei_set", 1)
                for l in range(len(LEVELS)):
                    for d in range(2):
                        b = slice(4 * d, 4 * d + 4)
                        if l:
                            wait("pe_y", 2 * (l - 1) + d + 1)
                        else:
                            wait("at_set", d + 1)
                        done(tt(LE[:, b, :], AT[:, b, :], level_mask(d, True, l + 1), ALU.mult), "lt_set")
                for d in range(2):
                    wait("pe_y", 2 * len(LEVELS) - 1 + d)
                    for q in SCAN[d][:3]:
                        i = tt(LE[:, 4 * d + q, :], kh[:, q, :], hp[:, EKD, q, d:d + 1].broadcast_to([P, P]), ALU.mult)
                    done(i, "kd_set")
                wait("oms_set", 1)
                done(tt(ors[:], oms[:], mhalf[:, 0:2], ALU.pow), "ors_set")

            nc.gpsimd.memset(mhalf[:], -0.5).then_inc(half_set, 1)
            pool.wait_ge(half_set, 1)
            rstd(0)
            rstd(1)
            add_out(0, GROUPS, (h_lat, h_ctx))
            rstd(2)
            rstd(3)
            pool.wait_ge(mk_in, 16)
            with pool.Fori(0, HEADS) as h:
                gdn(h)
            add_out(2, 1, (h_lat,))
            rstd(4)
            add_out(1, GROUPS, (h_lat,))
            rstd(5)


_INS = ["x", "c", "ctx", "c_ctx", "w_ada", "b_ada", "norm_g", "w_in", "conv_w", "a_log", "dt_bias",
        "o_norm_g", "w_pool", "pool_scale", "w_out", "ffn_w_in", "ffn_w_out", "final_g"]


def kernel(**inputs):
    import concourse.bacc as bacc
    from concourse.bass_utils import run_bass_kernel_spmd

    nc = bacc.Bacc("TRN2", target_bir_lowering=False, num_devices=1)
    arrays, args = {}, []
    given = {n: np.ascontiguousarray(inputs[n]) for n in _INS}
    given.update({"const_" + n: a for n, a in host_constants().items()})
    for name, a in given.items():
        arrays[f"in_{name}"] = a
        args.append(nc.dram_tensor(f"in_{name}", a.shape, mybir.dt.from_np(a.dtype), kind="ExternalInput").ap())
    args.append(nc.dram_tensor("out_0", (1, SEQ, D), F32, kind="ExternalOutput").ap())
    build(nc, *args)
    return run_bass_kernel_spmd(nc, [arrays], core_ids=[0]).results[0]["out_0"]
```

```python
from contextlib import ExitStack

import numpy as np

import concourse.bass as bass
from concourse import mybir

F32 = mybir.dt.float32
F32R = mybir.dt.float32r
ALU = mybir.AluOpType
ACT = mybir.ActivationFunctionType
ds = bass.ds

P = 128
D = 2048
KT = D // P
SEQ = 256
NTOK = 2 * SEQ
D_FF = 5632
GRID_W = 64
POOL_W = 1024
POOL_WINDOWS = (2, 4, 8, 16)
POOL_GROUP = POOL_W // len(POOL_WINDOWS)
HEADS = 8
DK = 128
COL_QKV = POOL_W
COL_BA = COL_QKV + 4 * HEADS * DK
N_BA = 4 * HEADS
N_MOD = 9
CONV_W = 4
CONV_LEFT = 2
EPS = 1e-6

TILE_K = 2
TILE_N = 512
TILE = TILE_K * TILE_N
RAW = 4
HL = 4
AHEAD = HL - 1
K_TILES = KT // TILE_K

ADA_N = 3 * D // TILE_N
ADA_TILES = ADA_N * K_TILES
HALF = 1024
PIECE0 = ADA_N * TILE_N // HALF
PIECES = (N_MOD - 3) * D // HALF
PB = HALF // P

GROUP_FF = 4
GROUPS = D_FF // (GROUP_FF * P)
PAIRS = GROUP_FF // 2
N_OUT = D // TILE_N
OUT_TILES = GROUP_FF // TILE_K
GROUP_TILES = PAIRS * K_TILES + N_OUT * OUT_TILES

SEGMENTS = ((0, 2 * D // HALF, 2), (2 * D // HALF, GROUPS, 1))
assert PIECES == GROUPS + 1

T_ADA = 0
T_FFN1 = T_ADA + ADA_TILES
T_HEADS = T_FFN1 + GROUPS * GROUP_TILES
T_POOL = T_HEADS + HEADS * K_TILES
T_WOUT = T_POOL + POOL_W // TILE_N * K_TILES
T_FFN2 = T_WOUT + N_OUT * K_TILES
T_END = T_FFN2 + GROUPS * GROUP_TILES


def transfers(t):
    if T_HEADS <= t < T_WOUT:
        return TILE_K
    base = T_FFN1 if t < T_HEADS else T_FFN2
    inside = base <= t and (t - base) % GROUP_TILES < PAIRS * K_TILES
    return TILE_K if inside else 1


LEVELS = (2, 4, 8, 16, 32, 64)
SCAN = ((2, 3, 0, 1), (3, 2, 1, 0))
BETA, G, GC, EG, NBEG, EGT, EKD = range(7)
PREP_G = 17


FAR = 1e4


def host_constants():
    quarter = D // 4
    omega = (1.0 / (10000.0 ** (np.arange(quarter, dtype=np.float32) / quarter))).astype(np.float32)
    t = np.arange(SEQ)
    er = (t // GRID_W).astype(np.float32)[:, None] * omega
    ec = (t % GRID_W).astype(np.float32)[:, None] * omega
    pos = np.concatenate([np.sin(er), np.cos(er), np.sin(ec), np.cos(ec)], axis=-1).astype(np.float32)
    i, j = np.arange(P)[:, None], np.arange(P)[None, :]
    ident = (i == j)
    levels = [((i // m) % 2 == 1) & (j // m == i // m - 1) for m in (1,) + LEVELS]
    masks = [FAR * (i <= j), FAR * (i >= j), i <= j, i >= j, np.ones((P, P))]
    masks += levels + [m.T for m in levels]
    masks = np.stack([m.astype(np.float32) for m in masks], axis=1).reshape(P, -1)
    pools = []
    for w in POOL_WINDOWS:
        lo, hi = np.clip(t - w // 2, 0, SEQ - 1), np.clip(t + w // 2 - 1, 0, SEQ - 1)
        inside = (t[None, :] >= lo[:, None]) & (t[None, :] <= hi[:, None])
        m = inside / (hi - lo + 1)[:, None] - np.eye(SEQ)
        pools.append(m.T.astype(np.float32))
    pools = np.stack(pools, axis=1)
    return {"pos": pos, "ident": ident.astype(np.float32), "masks": masks,
            "pools": np.ascontiguousarray(pools.reshape(SEQ, -1))}


MASKED, CUM, ONES, LEVEL = 0, 2, 4, 5
N_LEVEL = len(LEVELS) + 1
N_MASK = LEVEL + 2 * N_LEVEL


def build(nc, x, c, ctx, c_ctx, w_ada, b_ada, norm_g, w_in, conv_w, a_log, dt_bias, o_norm_g,
          w_pool, pool_scale, w_out, ffn_w_in, ffn_w_out, final_g, pos, ident_in, masks_in,
          pools_in, out):
    ada_rows = nc.dram_tensor("ada_rows", (2, 3 * D), F32, kind="Internal").ap()

    es = ExitStack()
    with es:
        def sb(name, shape, dt=F32, stack=es):
            return stack.enter_context(nc.sbuf_tensor(name, shape, dt))

        sems = {}

        def sem(name):
            sems[name] = es.enter_context(nc.semaphore(name))
            return sems[name]

        ps = es.enter_context(nc.psum_tensor("ps", [P, 8, 512], F32))

        xh = sb("xh", [P, KT, NTOK], F32R)
        xl = sb("xl", [P, KT, NTOK], F32R)
        h_lat = sb("h_lat", [P, 2, D])
        raw = sb("raw", [P, RAW, TILE])
        wh = sb("wh", [P, HL, TILE], F32R)
        wl = sb("wl", [P, HL, TILE], F32R)
        ident = sb("ident", [P, P])
        cols_a = sb("cols_a", [P, 64])
        cols_b = sb("cols_b", [P, 144])
        cT = sb("cT", [P, 2 * KT])
        cTh = sb("cTh", [P, 2 * KT], F32R)
        cTl = sb("cTl", [P, 2 * KT], F32R)
        adac = sb("adac", [P, 2, 1 + PIECES, PB])
        ones = sb("ones", [P, 1])
        cols_c = sb("cols_c", [P, 105])
        scale_c = sb("scale_c", [P, 5, KT])
        n_ss = sb("n_ss", [P, 2, 2])
        n_ms = sb("n_ms", [P, 2, 2])
        n_rstd = sb("n_rstd", [P, 2, 2])
        mhalf = sb("mhalf", [P, 8])

        with ExitStack() as st:
            h_ctx = sb("h_ctx", [P, 2, D], stack=st)
            gates = sb("gates", [P, 2, D], stack=st)
            with ExitStack() as first:
                crow = sb("crow", [32, P], stack=first)
                csil = sb("csil", [32, P], stack=first)
                arow = sb("arow", [2, 2, TILE_N], stack=first)
                brow = sb("brow", [2, 2, TILE_N], stack=first)
                rows_a = sb("rows_a", [64, P], stack=first)
                rows_b = sb("rows_b", [48, P], stack=first)
                rows_d = sb("rows_d", [96, P], stack=first)
                rows_c = sb("rows_c", [105, P], stack=first)
            with ExitStack() as norms:
                ub = sb("ub", [P, 2, 4, SEQ], stack=norms)
            sg = sb("sg", [P, 2, 512], stack=st)
            hf = sb("hf", [P, 2, 512], stack=st)
            tmp = sb("tmp", [P, 2, 512], stack=st)
            with ExitStack() as norms:
                xn = sb("xn", [P, 2, D], stack=norms)
                xc = sb("xc", [P, 2, D], stack=norms)
            hth = sb("hth", [P, GROUP_FF, 512], F32R, stack=st)
            htl = sb("htl", [P, GROUP_FF, 512], F32R, stack=st)
            acc = sb("acc", [P, 2, HALF], stack=st)
            abuf = sb("abuf", [P, 2, HALF], stack=st)
        yst = ExitStack()
        with yst:
            yg = sb("yg", [P, HEADS, SEQ], stack=yst)
            with ExitStack() as st:
                mk = sb("mk", [P, N_MASK, P], stack=st)
                gp = sb("gp", [P, 7, 4, 2 * HEADS], stack=st)
                hp = sb("hp", [P, 7, 4, 2], stack=st)
                cw = sb("cw", [P, 12], stack=st)
                pq = sb("pq", [P, SEQ + 4], stack=st)
                pk = sb("pk", [P, 2, SEQ + 4], stack=st)
                pv = sb("pv", [P, 2, SEQ + 4], stack=st)
                pz = sb("pz", [P, SEQ], stack=st)
                qT = sb("qT", [P, SEQ], stack=st)
                zs = sb("zs", [P, SEQ], stack=st)
                with ExitStack() as st2:
                    kT = sb("kT", [P, 2, SEQ], stack=st2)
                    vT = sb("vT", [P, 2, SEQ], stack=st2)
                AY = sb("AY", [P, 8, P], stack=st)
                with ExitStack() as st2:
                    wba = sb("wba", [P, KT, N_BA], stack=st2)
                    wbah = sb("wbah", [P, KT, N_BA], F32R, stack=st2)
                    wbal = sb("wbal", [P, KT, N_BA], F32R, stack=st2)
                    rowc = sb("rowc", [P, 2, 2 * HEADS], stack=st2)
                    baT = sb("baT", [N_BA, NTOK], stack=st2)
                    sp_t = sb("sp_t", [P, 6, 4, 2 * HEADS], stack=st2)
                AT = sb("AT", [P, 8, P], stack=st)
                X = sb("X", [P, 8, P], stack=st)
                XT = sb("XT", [P, 8, P], stack=st)
                LE = sb("LE", [P, 8, P], stack=st)
                Aq = sb("Aq", [P, 4, P], stack=st)
                AqT = sb("AqT", [P, 4, P], stack=st)
                kh = sb("kh", [P, 4, P], stack=st)
                khT = sb("khT", [P, 4, P], stack=st)
                vb = sb("vb", [P, 8, P], stack=st)
                S, o, vbp, vn = (X[:, 2 * i:2 * i + 2, :] for i in range(4))
                ssb = sb("ssb", [P, 6], stack=st)
                rs = sb("rs", [P, 6], stack=st)
                rq = sb("rq", [P, 2], stack=st)
                oss = sb("oss", [P, 2], stack=st)
                oms = sb("oms", [P, 2], stack=st)
                ors = sb("ors", [P, 2], stack=st)
            with ExitStack() as st:
                u = sb("u", [P, 2, POOL_W], stack=st)
                pg = sb("pg", [P, 2, 4, SEQ], stack=st)
                pT = sb("pT", [P, 8, SEQ], stack=st)
                wp = sb("wp", [P, 4, 2, POOL_GROUP], stack=st)
                yp = sb("yp", [P, 8, SEQ], stack=st)

        raw_in = [sem(f"raw_in{i}") for i in range(RAW)]
        hi_done, lo_done, tile_used = sem("hi_done"), sem("lo_done"), sem("tile_used")
        ada_evac = sem("ada_evac")
        brow_in = [sem("brow_in0"), sem("brow_in1")]
        arow_out = [sem("arow_out0"), sem("arow_out1")]
        c_in, c_silu, c_turned, c_cols = sem("c_in"), sem("c_silu"), sem("c_turned"), sem("c_cols")
        id_in, x_in = sem("id_in"), sem("x_in")
        rows_in, rows_turned, cols_done, scale_done = (
            sem("rows_in"), sem("rows_turned"), sem("cols_done"), sem("scale_done"))
        gates_in, fg_in = sem("gates_in"), sem("fg_in")
        half_set, h_set = sem("half_set"), sem("h_set")
        ss_done, ms_done, rstd_done, xn_done, x_turned, u_done, uh_done, x_ready = (
            sem("ss_done"), sem("ms_done"), sem("rstd_done"), sem("xn_done"), sem("x_turned"),
            sem("u_done"), sem("uh_done"), sem("x_ready"))
        F = []
        for f in range(2):
            F.append({n: sem(f"{n}{f}") for n in ("silu_done", "hf_done", "hh_done", "h_ready")})
        gated = [sem(f"gated{i}") for i in range(3)]
        added = [sem(f"added{i}") for i in range(3)]
        out_done = sem("out_done")
        mk_in, ba_in, rowc_in = sem("mk_in"), sem("ba_in"), sem("rowc_in")
        ba_hi, ba_split, ba_done, prep_dve, prep_act, prep_pe = (
            sem("ba_hi"), sem("ba_split"), sem("ba_done"), sem("prep_dve"), sem("prep_act"), sem("prep_pe"))
        margins_set = sem("margins_set")
        abuf_in = [sem("abuf_in0"), sem("abuf_in1")]
        acc_done, acc_zero, red_pe, red_out = sem("acc_done"), sem("acc_zero"), sem("red_pe"), sem("red_out")
        bias_done, gate_pe, gate_set, acc8_done = sem("bias_done"), sem("gate_pe"), sem("gate_set"), sem("acc8_done")
        ssc_done, xn2_done, fin_done = sem("ssc_done"), sem("xn2_done"), sem("fin_done")
        ones_set, bat_set = sem("ones_set"), sem("bat_set")
        pool_u, pool_p, pool_pe, pool_pe2, yp_done, y_hi, y_ready, pool_in = (
            sem("pool_u"), sem("pool_p"), sem("pool_pe"), sem("pool_pe2"), sem("yp_done"),
            sem("y_hi"), sem("y_ready"), sem("pool_in"))
        PER = dict(hp_set=1, cw_set=1, conv=12, act_in=4, squared=2, pe_v=1, pe_k=1, pe_ss=1,
                   ss_sb=1, rs_set=1, rq_set=1, kh_set=1, pe_kh=1, khT_set=1, vb_set=1, pe_g=1,
                   pe_cum=2, pe_qk=1, dd_set=2, e_set=2, ei_set=1, a_set=2, aq_set=1,
                   pe_at=2, pe_aqt=1, at_set=2, aqt_set=1, m1_set=2, mt_set=2, x1_set=4, lt_set=12,
                   pe_y=12, y_set=12, pe_zt=12, pe_z=10, x_set=10, xt_set=12, kd_set=2,
                   pe_r=6, vbp_set=6, pe_vn=8, vn_set=8, pe_kv=6, s_set=6, pe_av=4,
                   o_set=8, osc=1, oss_set=1, oms_set=1, ors_set=1, on_set=1, pe_o=1, y_done=1,
                   evac_act=2, evac_dve=2)
        HS = {n: sem("gdn_" + n) for n in PER}

        def at(name, h, k):
            return h * PER[name] + k

        block = es.enter_context(nc.Block())

        w_ada_v = w_ada[0].rearrange("(k p) n -> p k n", p=P)
        w_in_v = w_in[0].rearrange("(k p) n -> p k n", p=P)
        w_out_v = w_out[0].rearrange("(k p) n -> p k n", p=P)
        w_gu_v = [ffn_w_in[0, f].rearrange("(k p) (s n) -> p k s n", p=P, s=2) for f in range(2)]
        w_dn_v = [ffn_w_out[0, f].rearrange("(k p) n -> p k n", p=P) for f in range(2)]
        w_qkvz_v = w_in_v[:, :, COL_QKV:COL_BA].rearrange("p k (s n) -> p k s n", s=4)
        NTT = (NTOK // P, SEQ // P, SEQ // P)

        def tiles(r, per, t):
            return r * per + (t + 1)

        def loads(r, per, t):
            before = lambda n: 16 * sum(map(transfers, range(n % RAW, n + 1, RAW)))
            return r * (before(t + per) - before(t)) + before(t)

        def bc(ap, n):
            return ap.unsqueeze(1).broadcast_to([P, n, ap.shape[-1]])

        def mask(i, n=4):
            return bc(mk[:, i, :], n)

        def half(ap, m, d, transposed):
            return ap.rearrange("p n (a r m) -> p (n a) r m", r=2, m=m)[:, :, int((d == 1) != transposed), :]

        def level_mask(d, transposed, lvl):
            return mask(LEVEL + (N_LEVEL if (d == 1) != transposed else 0) + lvl)

        def acc_count(g, seg, tiles_):
            lo, _, n = SEGMENTS[seg]
            before = sum((hi_ - lo_) * KT * n_ for lo_, hi_, n_ in SEGMENTS[:seg])
            return g * (KT * n) + (before - lo * KT * n + n * tiles_ + 4)

        def seen(base, streams, b):
            return base + (b + 1 if streams == 1 else (3, 4, 7, 8)[b])

        @block.sync
        def _(sp):
            sp.sem_inc(ada_evac, 2)
            sp.sem_inc(arow_out[0], 16)
            sp.sem_inc(arow_out[1], 16)
            sp.sem_inc(lo_done, RAW)
            sp.sem_inc(tile_used, HL)
            for i in range(3):
                sp.sem_inc(gated[i], N_OUT * NTT[i])
                sp.sem_inc(added[i], 2)
            sp.sem_inc(HS["y_done"], 1)
            sp.sem_inc(acc_done, 4)

            def load(r, per, t, src):
                sp.wait_ge(lo_done, tiles(r, per, t))
                dst = raw[:, t % RAW, :].rearrange("p (k n) -> p k n", k=TILE_K)
                if transfers(t) == 1:
                    sp.dma_start(dst, src).then_inc(raw_in[t % RAW], 16)
                else:
                    for a in range(TILE_K):
                        block = dst[:, a]
                        if len(src.shape) == 4:
                            block = block.rearrange("p (s n) -> p s n", s=src.shape[2])
                        sp.dma_start(block, src[:, a]).then_inc(raw_in[t % RAW], 16)

            def ffn_loads(f, base):
                with sp.Fori(0, GROUPS) as g:
                    for j in range(GROUP_TILES):
                        if j < PAIRS * K_TILES:
                            p, k = divmod(j, K_TILES)
                            src = w_gu_v[f][:, TILE_K * k:TILE_K * (k + 1), :,
                                            ds(g * (GROUP_FF * P) + p * 2 * P, 2 * P)]
                        else:
                            n, k = divmod(j - PAIRS * K_TILES, OUT_TILES)
                            src = w_dn_v[f][:, ds(g * GROUP_FF + k * TILE_K, TILE_K),
                                            n * TILE_N:(n + 1) * TILE_N]
                        load(g, GROUP_TILES, base + j, src)

            with sp.Fori(0, ADA_N) as n:
                for k in range(K_TILES):
                    load(n, K_TILES, T_ADA + k,
                         w_ada_v[:, TILE_K * k:TILE_K * (k + 1), ds(n * TILE_N, TILE_N)])
            ffn_loads(0, T_FFN1)
            with sp.Fori(0, HEADS) as h:
                for k in range(K_TILES):
                    load(h, K_TILES, T_HEADS + k,
                         w_qkvz_v[:, TILE_K * k:TILE_K * (k + 1), :, ds(h * DK, DK)])
            with sp.Fori(0, POOL_W // TILE_N) as n:
                for k in range(K_TILES):
                    load(n, K_TILES, T_POOL + k,
                         w_in_v[:, TILE_K * k:TILE_K * (k + 1), ds(n * TILE_N, TILE_N)])
            with sp.Fori(0, N_OUT) as n:
                for k in range(K_TILES):
                    load(n, K_TILES, T_WOUT + k,
                         w_out_v[:, TILE_K * k:TILE_K * (k + 1), ds(n * TILE_N, TILE_N)])
            ffn_loads(1, T_FFN2)
            sp.wait_ge(out_done, 32)

        @block.tensor
        def _(pe):
            mm, turn = nc.tensor.matmul, nc.tensor.transpose

            def product(out, ah, al, bh, bl, first, last):
                mm(out, ah, bh, start=first, stop=False)
                mm(out, ah, bl, start=False, stop=False)
                return mm(out, al, bh, start=False, stop=last)

            def ada():
                pe.wait_ge(id_in, 16)
                pe.wait_ge(c_silu, 1)
                turn(ps[:, 2, 0:32], csil[:], ident[0:32, 0:32]).then_inc(c_turned, 1)
                pe.wait_ge(c_cols, 3)

                def block(r, b):
                    pe.wait_ge(ada_evac, r * 2 + (b + 1))
                    for j in range(K_TILES):
                        t = T_ADA + b * K_TILES + j
                        pe.wait_ge(lo_done, tiles(r, 2 * K_TILES, t) + RAW)
                        for a in range(TILE_K):
                            k = TILE_K * j + a
                            w = slice(a * TILE_N, (a + 1) * TILE_N)
                            i = product(ps[0:2, b, :], cTh[:, k:32:KT], cTl[:, k:32:KT],
                                        wh[:, t % HL, w], wl[:, t % HL, w], k == 0, k == KT - 1)
                        i.then_inc(tile_used, 1)

                last = ADA_N // 2 - 1
                with pe.Fori(0, last) as r:
                    for b in range(2):
                        block(r, b)
                block(last, 0)
                pe.wait_ge(rows_in, 16 * 7)
                turn(ps[:, 3, 0:64], rows_a[:], ident[0:64, 0:64])
                turn(ps[:, 3, 64:112], rows_b[:], ident[0:48, 0:48])
                turn(ps[:, 3, 112:208], rows_d[:], ident[0:96, 0:96])
                turn(ps[:, 3, 256:361], rows_c[:], ident[0:105, 0:105]).then_inc(rows_turned, 1)
                block(last, 1)
                pe.wait_ge(ada_evac, 2 + ADA_N)

            def norm(c, bufs, base):
                n = len(bufs)
                for rnd in range(2):
                    for s in range(n):
                        if rnd == 0:
                            pe.wait_ge(xn_done, c + s + 1)
                            pe.wait_ge(xn2_done, c + s + 1)
                            if s == 0:
                                pe.wait_ge(*((cols_done, 1) if c == 0 else (u_done, base)))
                        elif n == 2:
                            pe.wait_ge(u_done, base + 2 * (s + 1))
                        for k in range(8 * rnd, 8 * rnd + 8):
                            bank = 4 * s + k % 8 // 2 if n == 2 else k // 2
                            for t in range(2):
                                at_ = (k % 2) * SEQ + t * P
                                i = turn(ps[:, bank, at_:at_ + P], bufs[s][:, t, k * P:(k + 1) * P], ident[:])
                        i.then_inc(x_turned, 1)
                pe.wait_ge(u_done, base + (6 if n == 2 else 4))

            def reduce(streams, at_):
                for s in range(streams):
                    for b in range(PB):
                        i = mm(ps[:, at_, s * PB + b:s * PB + b + 1], acc[:, s, b * P:(b + 1) * P], ones[:],
                               start=True, stop=True)
                i.then_inc(red_pe, 1)

            def spread(piece, banks):
                for b in range(2 * PB):
                    i = mm(ps[:, banks[b // 4], (b % 4) * P:(b % 4 + 1) * P],
                           adac[:, 0, piece + b // PB, b % PB:b % PB + 1].broadcast_to([P, P]), ident[:],
                           start=True, stop=True)
                i.then_inc(gate_pe, 1)

            def ffn(f, base, nt, x_base):
                per = N_OUT * NTT[f]

                def group(g, seg):
                    for p in range(PAIRS):
                        pe.wait_ge(gated[f], g * per + (3 + p) * NTT[f])
                        if p == 1 and f == 0:
                            pe.wait_ge(red_out, g + 1)
                        for k in range(K_TILES):
                            t = base + p * K_TILES + k
                            if p == 0:
                                pe.wait_ge(x_ready, seen(x_base, 2 - f, k // 2))
                            pe.wait_ge(lo_done, tiles(g, GROUP_TILES, t) + RAW)
                            for a in range(TILE_K):
                                kk = TILE_K * k + a
                                for q in range(4):
                                    w = slice(a * TILE_N + q * P, a * TILE_N + (q + 1) * P)
                                    i = product(ps[:, 4 * p + q, 0:nt], wh[:, t % HL, w], wl[:, t % HL, w],
                                                xh[:, kk, 0:nt], xl[:, kk, 0:nt], kk == 0, kk == KT - 1)
                            i.then_inc(tile_used, 1)
                            if f == 0 and p == 0 and k == 1:
                                pe.wait_ge(u_done, 8)
                                pe.wait_ge(acc_zero, 1)
                                pe.wait_ge(acc_done, acc_count(g, seg, 0))
                                pe.wait_ge(gated[0], g * per + 4 * NTT[0])
                                reduce(2, 7)
                    for n in range(N_OUT):
                        if n < 2:
                            pe.wait_ge(F[f]["hf_done"], g * GROUP_FF + 2 * (n + 1))
                        else:
                            pe.wait_ge(gated[f], g * per + (per + (n - 1) * NTT[f]))
                        for k in range(OUT_TILES):
                            t = base + PAIRS * K_TILES + n * OUT_TILES + k
                            if n == 0:
                                pe.wait_ge(F[f]["h_ready"], g * GROUP_FF + TILE_K * (k + 1))
                            pe.wait_ge(lo_done, tiles(g, GROUP_TILES, t) + RAW)
                            for a in range(TILE_K):
                                kk = TILE_K * k + a
                                w = slice(a * TILE_N, (a + 1) * TILE_N)
                                for q in range(NTT[f]):
                                    x_ = slice(q * P, (q + 1) * P)
                                    i = product(ps[:, 4 * (n % 2) + q, :], hth[:, kk, x_], htl[:, kk, x_],
                                                wh[:, t % HL, w], wl[:, t % HL, w],
                                                kk == 0, kk == GROUP_FF - 1)
                            i.then_inc(tile_used, 1)

                if f == 0:
                    for seg, (lo, hi, _) in enumerate(SEGMENTS):
                        with pe.Fori(lo, hi) as g:
                            group(g, seg)
                else:
                    with pe.Fori(0, GROUPS) as g:
                        group(g, None)

            def token_tile(r, per, t, k, bank, part=range(TILE_K)):
                if part[0] == 0:
                    pe.wait_ge(lo_done, tiles(r, per, t) + RAW)
                for a in part:
                    kk = TILE_K * k + a
                    w = slice(a * TILE_N, (a + 1) * TILE_N)
                    for q in range(SEQ // P):
                        x_ = slice(q * P, (q + 1) * P)
                        i = product(ps[:, bank + q, :], xh[:, kk, x_], xl[:, kk, x_],
                                    wh[:, t % HL, w], wl[:, t % HL, w], kk == 0, kk == KT - 1)
                if part[-1] == TILE_K - 1:
                    i.then_inc(tile_used, 1)

            def head_tile(h, off, k, part=range(TILE_K)):
                t = T_HEADS + off * K_TILES + k
                if k == 0 and off and part[0] == 0:
                    pe.wait_ge(HS["evac_act"], at("evac_act", h, 2 * off))
                    pe.wait_ge(HS["evac_dve"], at("evac_dve", h, 2 * off))
                if part[0] == 0:
                    pe.wait_ge(lo_done, tiles(h, K_TILES, t) + RAW)
                for a in part:
                    kk = TILE_K * k + a
                    for q, nt in enumerate((SEQ, NTOK, NTOK, SEQ)):
                        w = slice(a * TILE_N + q * P, a * TILE_N + (q + 1) * P)
                        i = product(ps[:, q, 0:nt], wh[:, t % HL, w], wl[:, t % HL, w],
                                    xh[:, kk, 0:nt], xl[:, kk, 0:nt], kk == 0, kk == KT - 1)
                if part[-1] == TILE_K - 1:
                    i.then_inc(tile_used, 1)

            def decay_prep():
                pe.wait_ge(ba_split, 1)
                for k in range(KT):
                    i = product(ps[0:N_BA, 4, :], wbah[:, k, :], wbal[:, k, :], xh[:, k, :], xl[:, k, :],
                                k == 0, k == KT - 1)
                i.then_inc(ba_done, 1)

            def decay_turn():
                pe.wait_ge(bat_set, 1)
                for q in range(4):
                    i = turn(ps[:, 5, q * N_BA:(q + 1) * N_BA], baT[:, q * P:(q + 1) * P],
                             ident[0:N_BA, 0:N_BA])
                i.then_inc(ba_done, 1)

            def decay_sums():
                pe.wait_ge(prep_dve, PREP_G)
                pe.wait_ge(mk_in, 16)
                for q in range(4):
                    for d in range(2):
                        mm(ps[:, 6, q * 32 + 8 * d:q * 32 + 8 * d + 8], mk[:, CUM + d, :],
                           gp[:, G, q, 8 * d:8 * d + 8], start=True, stop=True)
                    i = mm(ps[:, 6, q * 32 + 16:q * 32 + 32], mk[:, ONES, :], gp[:, G, q, :],
                           start=True, stop=True)
                i.then_inc(prep_pe, 1)

            def gdn(h, block_of, next_of):
                def done(i, name):
                    i.then_inc(HS[name], 1)

                def wait(name, k):
                    pe.wait_ge(HS[name], at(name, h, k))

                def fill(*blocks):
                    for b in blocks:
                        block_of(b // TILE_K, b % TILE_K)

                def blk(bank, b):
                    return ps[:, bank, b * P:(b + 1) * P]

                wait("act_in", 1)
                for q in range(4):
                    i = turn(blk(5, q), kT[:, q // 2, (q % 2) * P:(q % 2 + 1) * P], ident[:])
                done(i, "pe_k")
                fill(2)
                wait("y_done", 1)
                wait("act_in", 2)
                for q in range(4):
                    i = turn(blk(4, q), vT[:, q // 2, (q % 2) * P:(q % 2 + 1) * P], ident[:])
                done(i, "pe_v")
                wait("squared", 2)
                for q in range(6):
                    i = mm(ps[:, 6, q:q + 1], AT[:, q, :], mk[:, ONES, 0:1], start=True, stop=True)
                done(i, "pe_ss")
                fill(3, 4)
                wait("kh_set", 1)
                for q in range(4):
                    i = turn(blk(7, q), kh[:, q, :], ident[:])
                done(i, "pe_kh")
                fill(5)
                wait("khT_set", 1)
                for q in range(4):
                    i = mm(blk(5, q), khT[:, q, :], khT[:, q, :], start=True, stop=True)
                done(i, "pe_g")
                wait("hp_set", 1)
                wait("vb_set", 1)
                for d in range(2):
                    for q in range(4):
                        i = mm(blk(4 + 2 * d, q), hp[:, G, q, d:d + 1].broadcast_to([P, P]),
                               mk[:, CUM + d, :], start=True, stop=True)
                    done(i, "pe_cum")
                wait("act_in", 3)
                for q in range(2):
                    i = mm(blk(7, q), qT[:, q * P:(q + 1) * P], khT[:, q, :], start=True, stop=True)
                done(i, "pe_qk")
                fill(6, 7)
                for d in range(2):
                    wait("a_set", d + 1)
                    for q in range(4):
                        i = turn(blk(4 + 2 * d, q), AY[:, 4 * d + q, :], ident[:])
                    done(i, "pe_at")
                wait("aq_set", 1)
                for q in range(4):
                    i = turn(blk(5, q), Aq[:, q, :], ident[:])
                done(i, "pe_aqt")
                fill(8)
                last = len(LEVELS) - 1
                for l in range(last + 1):
                    for d in range(2):
                        wait("lt_set", 2 * l + d + 1)
                        if l == 0:
                            wait("x1_set", d + 1)
                        else:
                            wait("x_set", 2 * (l - 1) + d + 1)
                        for q in range(4):
                            i = mm(blk(4 + 2 * d, q), LE[:, 4 * d + q, :], X[:, 4 * d + q, :],
                                   start=True, stop=True)
                        done(i, "pe_y")
                    for d in range(2):
                        wait("y_set", 2 * l + d + 1)
                        if l == 0:
                            wait("x1_set", 3 + d)
                            wait("aqt_set", 1)
                        else:
                            wait("xt_set", 2 * (l - 1) + d + 1)
                        m = LEVELS[l]

                        def part(bank):
                            return ps[:, bank, q * (P // 2):(q + 1) * (P // 2)].rearrange(
                                "p (a m) -> p a m", m=m)

                        if l < last:
                            for q in range(4):
                                v_ = slice(4 * d + q, 4 * d + q + 1)
                                i = mm(part(4 + 2 * d), XT[:, 4 * d + q, :], half(AY[:, v_, :], m, d, False),
                                       start=True, stop=True)
                            done(i, "pe_z")
                        for q in range(4):
                            v_ = slice(4 * d + q, 4 * d + q + 1)
                            i = mm(part(5 + 2 * d), AY[:, 4 * d + q, :], half(XT[:, v_, :], m, d, True),
                                   start=True, stop=True)
                        done(i, "pe_zt")
                for s in range(4):
                    for d in range(2):
                        q = SCAN[d][s]
                        if s:
                            wait("s_set", 2 * (s - 1) + d + 1)
                            i = mm(blk(4 + 2 * d, 0), khT[:, q, :], S[:, d, :], start=True, stop=True)
                            if s >= 2:
                                if s == 3:
                                    wait("o_set", 3 + d)
                                i = mm(blk(5 + 2 * d, 0), qT[:, q * P:(q + 1) * P], S[:, d, :],
                                       start=True, stop=True)
                            done(i, "pe_r")
                    fill(9 + 2 * s)
                    for d in range(2):
                        q = SCAN[d][s]
                        if s:
                            wait("vbp_set", 2 * (s - 1) + d + 1)
                            rhs = vbp[:, d, :]
                        else:
                            wait("xt_set", 2 * last + d + 1)
                            rhs = vb[:, 4 * d + q, :]
                        i = mm(blk(4 + 2 * d, 1), XT[:, 4 * d + q, :], rhs, start=True, stop=True)
                        done(i, "pe_vn")
                    if s < 3:
                        fill(10 + 2 * s)
                    for d in range(2):
                        q = SCAN[d][s]
                        wait("vn_set", 2 * s + d + 1)
                        if s < 3:
                            if s == 0:
                                wait("kd_set", d + 1)
                            i = mm(blk(4 + 2 * d, 2), LE[:, 4 * d + q, :], vn[:, d, :],
                                   start=True, stop=True)
                            done(i, "pe_kv")
                        if s >= 2:
                            wait("o_set", 4 * (s - 2) + d + 1)
                            i = mm(blk(5 + 2 * d, 1), AqT[:, 2 * d + q, :], vn[:, d, :],
                                   start=True, stop=True)
                            done(i, "pe_av")
                if next_of is not None:
                    for a in range(TILE_K):
                        next_of(a)
                wait("on_set", 1)
                for q in range(2):
                    i = turn(blk(4, q), o[:, q, :], ident[:])
                done(i, "pe_o")

            ada()
            norm(0, (xn, xc), 0)
            ffn(0, T_FFN1, NTOK, 0)
            pe.wait_ge(acc_done, acc_count(GROUPS - 1, len(SEGMENTS) - 1, KT))
            pe.wait_ge(gated[0], GROUPS * N_OUT * NTT[0] + N_OUT * NTT[0])
            reduce(1, 7)
            pe.wait_ge(red_out, GROUPS + 1)
            norm(2, (xn, xc), 8)
            for k in range(K_TILES):
                pe.wait_ge(x_ready, seen(8, 2, k // 2))
                head_tile(0, 0, k)
                if k == 3:
                    pe.wait_ge(u_done, 16)
            decay_prep()
            decay_turn()
            head_tile(0, 1, 0)
            decay_sums()
            with pe.Fori(0, HEADS - 2) as h:
                gdn(h, lambda k, a: head_tile(h, 1, k, (a,)), lambda a: head_tile(h, 2, 0, (a,)))

            def pool_block(k, a):
                if (k, a) == (0, 0):
                    pe.wait_ge(HS["evac_act"], 2 * HEADS)
                    pe.wait_ge(HS["evac_dve"], 2 * HEADS)
                token_tile(0, 0, T_POOL + k, k, 0, (a,))

            gdn(HEADS - 2, lambda k, a: head_tile(HEADS - 2, 1, k, (a,)), lambda a: pool_block(0, a))
            gdn(HEADS - 1, pool_block, None)
            for k in range(K_TILES):
                token_tile(0, 0, T_POOL + K_TILES + k, k, 2)
            pe.wait_ge(pool_u, 4)
            pe.wait_ge(pool_in, 16 * 3)
            pe.wait_ge(HS["y_done"], 1 + HEADS)
            for c_ in range(8):
                for q in range(2):
                    i = mm(ps[:, 4 + c_ // 2, (c_ % 2) * SEQ:(c_ % 2 + 1) * SEQ],
                           u[:, q, c_ * P:(c_ + 1) * P], pg[:, q, c_ // 2, :],
                           start=(q == 0), stop=(q == 1))
            i.then_inc(pool_pe, 1)
            pe.wait_ge(pool_p, 4)
            for c_ in range(8):
                for q in range(2):
                    i = mm(ps[:, c_ // 2, (c_ % 2) * SEQ:(c_ % 2 + 1) * SEQ],
                           wp[:, c_ // 2, q, (c_ % 2) * P:(c_ % 2 + 1) * P],
                           pT[:, c_ // 2 * 2 + q, :], start=(q == 0), stop=(q == 1))
            i.then_inc(pool_pe2, 1)
            spread(5, (4, 5, 6, 7))
            pe.wait_ge(y_ready, 2)
            pe.wait_ge(gate_set, 1)
            with pe.Fori(0, N_OUT // 2) as r:
                for n in range(2):
                    pe.wait_ge(gated[2], r * (2 * NTT[2]) + (n + 1) * NTT[2] + 2 * NTT[2])
                    for k in range(K_TILES):
                        token_tile(r, 2 * K_TILES, T_WOUT + n * K_TILES + k, k, 4 * n)
            pe.wait_ge(acc8_done, KT)
            reduce(1, 2)
            pe.wait_ge(red_out, GROUPS + 2)
            spread(11, (2, 3, 6, 7))
            pe.wait_ge(gate_set, 2)
            norm(4, (xn,), 16)
            ffn(1, T_FFN2, SEQ, 16)

        @block.scalar
        def _(act):
            fn = nc.scalar.activation

            def split(r, per, t):
                if t >= T_END:
                    return
                act.wait_ge(raw_in[t % RAW], loads(r, per, t))
                act.wait_ge(tile_used, tiles(r, per, t))
                nc.scalar.copy(wh[:, t % HL, :], raw[:, t % RAW, :]).then_inc(hi_done, 1)

            def bias_in(r, b):
                act.dma_start(brow[:, b % 2, :], b_ada[0:1, ds(r * (2 * TILE_N) + b * TILE_N, TILE_N)]
                              .broadcast_to([2, TILE_N])).then_inc(brow_in[b % 2], 16)

            def start():
                act.dma_start(ident[:], ident_in).then_inc(id_in, 16)
                act.dma_start(crow[0:16, :], c.rearrange("b (k p) -> (b k) p", p=P)).then_inc(c_in, 16)
                act.dma_start(crow[16:32, :], c_ctx.rearrange("(k p) -> k p", p=P)).then_inc(c_in, 16)
                act.dma_start(h_lat[:], x[0].rearrange("(t p) n -> p t n", p=P)).then_inc(x_in, 16)
                act.dma_start(h_ctx[:], ctx[0].rearrange("(t p) n -> p t n", p=P)).then_inc(x_in, 16)
                act.dma_start(gates[:], pos.rearrange("(t p) n -> p t n", p=P)).then_inc(x_in, 16)
                for b in range(2):
                    bias_in(0, b)
                act.dma_start(rows_d[:], b_ada[:, 3 * D:].rearrange("b (k p) -> (b k) p", p=P)).then_inc(rows_in, 16)
                act.dma_start(rows_b[:], norm_g[0].rearrange("n (k p) -> (n k) p", p=P)).then_inc(rows_in, 16)
                act.dma_start(rows_c[0:96, :], conv_w[0].rearrange("j (r p) -> (j r) p", p=P)).then_inc(rows_in, 16)
                act.dma_start(rows_c[96:104, :], pool_scale[0].rearrange("(k p) -> k p", p=P)).then_inc(rows_in, 16)
                act.dma_start(rows_c[104:105, :], o_norm_g).then_inc(rows_in, 16)
                act.wait_ge(c_in, 32)
                fn(csil[:], crow[:], ACT.Silu).then_inc(c_silu, 1)

            def ada():
                def row_out(r, b):
                    act.wait_ge(ada_evac, r * 2 + (b + 3))
                    act.dma_start(ada_rows[:, ds(r * (2 * TILE_N) + b * TILE_N, TILE_N)],
                                  arow[:, b % 2, :]).then_inc(arow_out[b % 2], 16)

                def block(r, b, steps={}):
                    for k in range(K_TILES):
                        if isinstance(r, int):
                            split(0, 0, T_ADA + (2 * r + b) * K_TILES + k + AHEAD)
                        else:
                            split(r, 2 * K_TILES, T_ADA + b * K_TILES + k + AHEAD)
                        if k == 2 and not (isinstance(r, int) and r == b == 0):
                            row_out(r, b - 1)
                            if not isinstance(r, int) or 2 * r + b + 1 < ADA_N:
                                bias_in(r, b + 1)
                        if k in steps:
                            steps[k]()

                def rows_written(n):
                    for b in range(2):
                        act.wait_ge(arow_out[b], 16 * (1 + n // 2))

                def squares(t):
                    act.wait_ge(h_set, 1)
                    mean_square(h_lat, t)

                for t in range(AHEAD):
                    split(0, 0, T_ADA + t)
                block(0, 0)
                block(0, 1)
                block(1, 0, {1: lambda: squares(0), 4: lambda: squares(1)})
                block(1, 1, {1: lambda: scale_first(0, xn, h_lat), 4: lambda: scale_first(1, xc, h_ctx)})
                n_cols = 2 * D // TILE_N
                with act.Fori(2, n_cols // 2) as r:
                    for b in range(2):
                        block(r, b)
                block(n_cols // 2, 0)
                rows_written(n_cols)
                rows = ada_rows.rearrange("s (k p) -> s k p", p=P)
                for s in range(2):
                    act.dma_start(rows_a[32 * s:32 * s + 32, :], rows[s, 0:32, :]).then_inc(rows_in, 16)
                for n in range(n_cols + 1, ADA_N):
                    block(n // 2, n % 2)
                row_out(ADA_N // 2, -1)
                rows_written(ADA_N)
                act.wait_ge(h_set, 1)
                for s in range(2):
                    act.dma_start(gates[:, s, :], ada_rows[s:s + 1, 2 * D:3 * D].broadcast_to([P, D])
                                  ).then_inc(gates_in, 16)

            def mean_square(src, t):
                fn(xn[:, t, :], src[:, t, :], ACT.Square, accum_out=n_ss[:, 0, t:t + 1]).then_inc(ss_done, 1)

            def mean_squares(src):
                for t in range(2):
                    mean_square(src, t)

            def scale_first(c_, dst, src):
                act.wait_ge(rstd_done, c_ + 1)
                fn(dst[:, 0, :], src[:, 0, :], ACT.Copy, scale=n_rstd[:, c_ % 2, 0:1]).then_inc(xn_done, 1)

            def modulate_(c_, n, base):
                act.wait_ge(scale_done, (2, 4, 5)[c_ // 2])
                shift = (cols_a[:, 0:16], cols_a[:, 32:48], adac[:, 0, 1:3].rearrange("p a b -> p (a b)"),
                         adac[:, 1, 1:3].rearrange("p a b -> p (a b)"),
                         adac[:, 0, 7:9].rearrange("p a b -> p (a b)"))
                j = base
                for rnd in range(2):
                    for s in range(n):
                        act.wait_ge(x_turned, base // 2 + rnd * n + s + 1)
                        for k in range(8 * rnd, 8 * rnd + 8):
                            bank = 4 * s + k % 8 // 2 if n == 2 else k // 2
                            if k % 4 == 0 and j >= 2:
                                act.wait_ge(x_ready, j - 1)
                            i = fn(ub[:, j % 2, k % 4, :], ps[:, bank, (k % 2) * SEQ:(k % 2 + 1) * SEQ],
                                   ACT.Identity, bias=shift[c_ + s][:, k:k + 1],
                                   scale=scale_c[:, c_ + s, k:k + 1])
                            if k % 4 == 3:
                                i.then_inc(u_done, 1)
                                j += 1

            def load_piece(i, col, sem_, count):
                act.wait_ge(sem_, count)
                act.dma_start(abuf[:, i % 2, :], w_ada_v[:, i, ds(col, HALF)]).then_inc(abuf_in[i % 2], 16)

            def hidden(f, g, base, p, nt):
                s = F[f]
                act.wait_ge(tile_used, tiles(g, GROUP_TILES, base + (p + 1) * K_TILES - 1) + HL)
                for b in range(2):
                    fn(sg[:, b, 0:nt], ps[:, 4 * p + b, 0:nt], ACT.Silu).then_inc(s["silu_done"], 1)
                for b in range(2):
                    act.wait_ge(s["hf_done"], g * GROUP_FF + (2 * p + b + 1))
                    nc.scalar.copy(hth[:, 2 * p + b, 0:nt], hf[:, b, 0:nt]).then_inc(s["hh_done"], 1)

            def ffn(f, base, nt):
                def group(g, r, per, t0, seg):
                    for j in range(GROUP_TILES):
                        split(r, per, t0 + j + AHEAD)
                        if seg is not None and j < KT:
                            load_piece(j, g * HALF + PIECE0 * HALF, acc_done, acc_count(g, seg, max(j - 1, 0)))
                        if j in (K_TILES - 1, 2 * K_TILES - 1):
                            hidden(f, g, base, j // K_TILES, nt)
                if f == 0:
                    for seg, (lo, hi, _) in enumerate(SEGMENTS):
                        with act.Fori(lo, hi) as g:
                            group(g, g, GROUP_TILES, base, seg)
                else:
                    with act.Fori(0, GROUPS - 1) as g:
                        group(g, g, GROUP_TILES, base, None)
                    group(GROUPS - 1, 0, 0, base + (GROUPS - 1) * GROUP_TILES, None)

            def head_out(h, off):
                act.wait_ge(tile_used, tiles(h, K_TILES, T_HEADS + (off + 1) * K_TILES - 1) + HL)
                for b, dst in ((1, pk), (2, pv)):
                    nc.scalar.copy(dst[:, :, CONV_LEFT:CONV_LEFT + SEQ],
                                   ps[:, b, :].rearrange("p (s n) -> p s n", s=2)).then_inc(HS["evac_act"], 1)

            def decay_prep():
                act.wait_ge(prep_dve, 1)
                act.wait_ge(rowc_in, 32)
                ba = ps[:, 5, 0:4 * N_BA].rearrange("p (t n) -> p t n", t=4)
                fn(gp[:, BETA], ba[:, :, 0:16], ACT.Sigmoid).then_inc(prep_act, 1)
                fn(rowc[:, 1, :], rowc[:, 1, :], ACT.Exp).then_inc(prep_act, 1)
                act.wait_ge(prep_dve, 2)
                fn(sp_t[:, 1], sp_t[:, 1], ACT.Exp, scale=-1.0).then_inc(prep_act, 1)
                act.wait_ge(prep_pe, 1)
                sums = ps[:, 6, 0:128].rearrange("p (t n) -> p t n", t=4)
                fn(gp[:, EG], sums[:, :, 0:16], ACT.Exp).then_inc(prep_act, 1)
                fn(gp[:, EGT], sums[:, :, 16:32], ACT.Exp).then_inc(prep_act, 1)
                act.wait_ge(prep_dve, PREP_G + 2)
                fn(gp[:, EKD], gp[:, EKD], ACT.Exp).then_inc(prep_act, 1)

            def gdn(h, point, tail):
                def done(i, name):
                    i.then_inc(HS[name], 1)

                def wait(name, k):
                    act.wait_ge(HS[name], at(name, h, k))

                def quad(bank):
                    return ps[:, bank, :].rearrange("p (q n) -> p q n", q=4)

                point(0)
                wait("conv", CONV_W)
                done(fn(kT[:], kT[:], ACT.Silu), "act_in")
                wait("act_in", 1)
                done(fn(AT[:, 0:4, :].rearrange("p a b -> p (a b)"), kT[:].rearrange("p a b -> p (a b)"), ACT.Square), "squared")
                wait("conv", 2 * CONV_W)
                done(fn(vT[:], vT[:], ACT.Silu), "act_in")
                wait("conv", 3 * CONV_W)
                done(fn(qT[:], qT[:], ACT.Silu), "act_in")
                wait("act_in", 3)
                done(fn(AT[:, 4:6, :].rearrange("p a b -> p (a b)"), qT[:], ACT.Square), "squared")
                wait("evac_dve", 2)
                done(fn(zs[:], pz[:], ACT.Silu), "act_in")
                point(1)
                wait("pe_v", 1)
                wait("hp_set", 1)
                for v_ in range(8):
                    i = fn(vb[:, v_, :], ps[:, 4, (v_ % 4) * P:(v_ % 4 + 1) * P], ACT.Copy,
                           scale=hp[:, BETA, v_ % 4, v_ // 4:v_ // 4 + 1])
                done(i, "vb_set")
                point(2)
                wait("pe_kh", 1)
                done(nc.scalar.copy(khT[:], quad(7)), "khT_set")
                point(3)
                for d in range(2):
                    wait("dd_set", d + 1)
                    done(fn(LE[:, 4 * d:4 * d + 4, :], LE[:, 4 * d:4 * d + 4, :], ACT.Exp, scale=-1.0), "e_set")
                for d in range(2):
                    wait("pe_at", d + 1)
                    done(nc.scalar.copy(AT[:, 4 * d:4 * d + 4, :], quad(4 + 2 * d)), "at_set")
                wait("pe_aqt", 1)
                done(nc.scalar.copy(AqT[:], quad(5)), "aqt_set")
                point(4)
                for l in range(len(LEVELS)):
                    for d in range(2):
                        wait("pe_y", 2 * l + d + 1)
                        done(nc.scalar.copy(AY[:, 4 * d:4 * d + 4, :], quad(4 + 2 * d)), "y_set")
                for s in range(4):
                    for d in range(2):
                        wait("pe_vn", 2 * s + d + 1)
                        done(nc.scalar.copy(vn[:, d, :], ps[:, 4 + 2 * d, P:2 * P]), "vn_set")
                    if s < 3:
                        point(5 + s)
                tail()
                wait("osc", 1)
                for q in range(2):
                    i = fn(vbp[:, q, :], o[:, q, :], ACT.Square, accum_out=oss[:, q:q + 1])
                done(i, "oss_set")

            start()
            ada()
            modulate_(0, 2, 0)
            ffn(0, T_FFN1, NTOK)
            act.wait_ge(added[0], GROUPS * N_OUT * NTT[0] + 2)
            mean_squares(h_lat)
            scale_first(2, xn, h_lat)
            scale_first(3, xc, h_ctx)
            modulate_(2, 2, 8)
            act.wait_ge(x_ready, 16)
            act.dma_start(wba[:], w_in_v[:, :, COL_BA:COL_BA + N_BA]).then_inc(ba_in, 16)
            act.dma_start(rowc[:, 0, :], dt_bias.rearrange("l d h -> l (d h)").broadcast_to([P, 16])).then_inc(rowc_in, 16)
            act.dma_start(rowc[:, 1, :], a_log.rearrange("l d h -> l (d h)").broadcast_to([P, 16])).then_inc(rowc_in, 16)
            act.dma_start(mk[:], masks_in.rearrange("p (m n) -> p m n", n=P)).then_inc(mk_in, 16)
            for k in range(K_TILES):
                split(0, 0, T_HEADS + k + AHEAD)
            act.wait_ge(ba_in, 16)
            nc.scalar.copy(wbah[:], wba[:]).then_inc(ba_hi, 1)
            head_out(0, 0)
            decay_prep()
            with act.Fori(0, HEADS - 1) as h:
                gdn(h, lambda k: split(h, K_TILES, T_HEADS + K_TILES + k + AHEAD), lambda: head_out(h, 1))
            gdn(HEADS - 1, lambda k: split(0, 0, T_POOL + k + AHEAD), lambda: None)
            act.wait_ge(HS["y_done"], HEADS + 1)
            act.dma_start(pg[:], pools_in.rearrange("(t p) (g n) -> p t g n", p=P, g=4)).then_inc(pool_in, 16)
            for s in range(2):
                act.dma_start(wp[:, 2 * s:2 * s + 2], w_pool[0, 2 * s:2 * s + 2].rearrange("g (t p) n -> p g t n", p=P)
                              ).then_inc(pool_in, 16)
            for q in range(2):
                nc.scalar.copy(u[:, q, 0:TILE_N], ps[:, q, :]).then_inc(pool_u, 1)
            for k in range(K_TILES):
                split(0, 0, T_POOL + K_TILES + k + AHEAD)
            act.wait_ge(tile_used, T_WOUT + HL)
            for q in range(2):
                nc.scalar.copy(u[:, q, TILE_N:2 * TILE_N], ps[:, 2 + q, :]).then_inc(pool_u, 1)
            act.wait_ge(pool_pe, 1)
            for b in range(2):
                nc.scalar.copy(pT[:, 2 * b:2 * b + 2, :].rearrange("p a b -> p (a b)"), ps[:, 4 + b, :]
                               ).then_inc(pool_p, 1)
            act.wait_ge(pool_pe2, 1)
            for c_ in range(8):
                i = fn(yp[:, c_, :], ps[:, c_ // 2, (c_ % 2) * SEQ:(c_ % 2 + 1) * SEQ], ACT.Copy,
                       scale=cols_c[:, 96 + c_:97 + c_])
            i.then_inc(yp_done, 1)
            act.wait_ge(y_ready, 2)

            def gate_rows(s, banks):
                act.wait_ge(gate_pe, s + 1)
                for b in range(4):
                    i = nc.scalar.copy(gates[:, s, b * 512:(b + 1) * 512], ps[:, banks[b], :])
                i.then_inc(gate_set, 1)

            gate_rows(0, (4, 5, 6, 7))
            for k in range(N_OUT * K_TILES):
                split(0, 0, T_WOUT + k + AHEAD)
                if k % 2 == 0:
                    i = k // 2
                    if i < 2:
                        load_piece(i, (PIECE0 + GROUPS) * HALF, y_ready, 2)
                    else:
                        load_piece(i, (PIECE0 + GROUPS) * HALF, acc8_done, i - 1)
            gate_rows(1, (2, 3, 6, 7))
            act.wait_ge(added[2], N_OUT * NTT[2] + 2)
            act.dma_start(gates[:, 0, :], final_g.unsqueeze(0).broadcast_to([P, D])).then_inc(fg_in, 16)
            mean_squares(h_lat)
            scale_first(4, xn, h_lat)
            modulate_(4, 1, 16)
            ffn(1, T_FFN2, SEQ)
            act.wait_ge(added[1], GROUPS * N_OUT * NTT[1] + 2)
            mean_squares(h_lat)
            for t in range(2):
                act.wait_ge(fin_done, t + 1)
                act.dma_start(out[0].rearrange("(t p) n -> p t n", p=P)[:, t, :], xn[:, t, :]).then_inc(out_done, 16)

        @block.vector
        def _(dve):
            V = nc.vector
            tt, ts, stt = V.tensor_tensor, V.tensor_scalar, V.scalar_tensor_tensor

            def split(r, per, t):
                if t >= T_END:
                    return
                dve.wait_ge(hi_done, tiles(r, per, t))
                tt(wl[:, t % HL, :], raw[:, t % RAW, :], wh[:, t % HL, :].bitcast(F32), ALU.subtract
                   ).then_inc(lo_done, 1)

            def ada():
                dve.wait_ge(c_turned, 1)
                V.tensor_copy(cT[:], ps[:, 2, 0:32]).then_inc(c_cols, 1)
                dve.wait_ge(c_cols, 1)
                V.tensor_copy(cTh[:], cT[:]).then_inc(c_cols, 1)
                dve.wait_ge(c_cols, 2)
                tt(cTl[:], cT[:], cTh[:].bitcast(F32), ALU.subtract).then_inc(c_cols, 1)
                V.memset(ones[:], 1.0).then_inc(ones_set, 1)

                def evacuate(r, b):
                    dve.wait_ge(tile_used, tiles(r, 2 * K_TILES, T_ADA + b * K_TILES + K_TILES - 1) + HL)
                    turn_ = r * 16 + (16 if b >= 0 else 0)
                    dve.wait_ge(brow_in[b % 2], turn_)
                    dve.wait_ge(arow_out[b % 2], turn_)
                    tt(arow[:, b % 2, :], ps[0:2, b % 2, :], brow[:, b % 2, :], ALU.add).then_inc(ada_evac, 1)

                def block(r, b, steps={}):
                    for k in range(K_TILES):
                        if isinstance(r, int):
                            split(0, 0, T_ADA + (2 * r + b) * K_TILES + k + AHEAD)
                        else:
                            split(r, 2 * K_TILES, T_ADA + b * K_TILES + k + AHEAD)
                        if k == 0 and not (isinstance(r, int) and r == b == 0):
                            evacuate(r, b - 1)
                        if k in steps:
                            steps[k]()

                def to_columns():
                    dve.wait_ge(rows_turned, 1)
                    V.tensor_copy(cols_a[:], ps[:, 3, 0:64])
                    V.tensor_copy(cols_b[:], ps[:, 3, 64:208])
                    V.tensor_copy(cols_c[:], ps[:, 3, 256:361]).then_inc(cols_done, 1)
                    dve.wait_ge(cols_done, 1)
                    scales(0, ((cols_a[:, 16:32], 0), (cols_a[:, 48:64], 0)))

                def squares(t):
                    dve.wait_ge(x_in, 48)
                    square_context(t)

                def rstds():
                    rstd(0)
                    rstd(1)

                for t in range(AHEAD):
                    split(0, 0, T_ADA + t)
                last = ADA_N // 2 - 1
                block(0, 0)
                block(0, 1)
                block(1, 0, {2: lambda: squares(0), 5: lambda: squares(1)})
                block(1, 1, {0: rstds, 2: lambda: scale_second(0, 0), 5: lambda: scale_second(0, 1)})
                with dve.Fori(2, last) as r:
                    for b in range(2):
                        block(r, b)
                block(last, 0)
                block(last, 1, {4: to_columns})
                evacuate(last, 1)

            def scales(first, parts):
                for i, (sc_, n) in enumerate(parts):
                    stt(scale_c[:, first + i, :], sc_, 1.0, cols_b[:, KT * n:KT * (n + 1)], ALU.add, ALU.mult
                        ).then_inc(scale_done, 1)

            def rstd(c_):
                s = c_ % 2 if c_ < 4 else 0
                dve.wait_ge(ssc_done if s else ss_done, 2 * (c_ // 2 + 1) if c_ < 5 else 8)
                ts(n_ms[:, s], n_ss[:, s], 1.0 / D, EPS, ALU.mult, ALU.add).then_inc(ms_done, 1)

            def square_context(t):
                V.tensor_tensor_reduce(out=xc[:, t, :], in0=h_ctx[:, t, :], in1=h_ctx[:, t, :],
                                       scale=1.0, scalar=0.0, op0=ALU.mult, op1=ALU.add,
                                       accum_out=n_ss[:, 1, t:t + 1]).then_inc(ssc_done, 1)

            def scale_second(c_, s):
                dve.wait_ge(rstd_done, c_ + s + 1)
                dst, src = ((xn, h_lat), (xc, h_ctx))[s]
                ts(dst[:, 1, :], src[:, 1, :], n_rstd[:, s, 1:2], None, ALU.mult).then_inc(xn2_done, 1)

            def scale(c_, both):
                if both:
                    for t in range(2):
                        square_context(t)
                for s in range(1 + both):
                    rstd(c_ + s)
                for s in range(1 + both):
                    scale_second(c_, s)

            def split_x(base, n):
                j = base
                for rnd in range(2):
                    for s in range(n):
                        for b in range(2 * rnd, 2 * rnd + 2):
                            k, cols = slice(4 * b, 4 * b + 4), slice(s * SEQ, (s + 1) * SEQ)
                            dve.wait_ge(u_done, j + 1)
                            V.tensor_copy(xh[:, k, cols], ub[:, j % 2]).then_inc(uh_done, 1)
                            dve.wait_ge(uh_done, j + 1)
                            tt(xl[:, k, cols], ub[:, j % 2], xh[:, k, cols].bitcast(F32), ALU.subtract
                               ).then_inc(x_ready, 1)
                            j += 1

            def piece(i, streams, arrived, sem_, count):
                dve.wait_ge(abuf_in[i % 2], arrived)
                for s in range(streams):
                    c_ = cT[:, KT * s + i:KT * s + i + 1]
                    if i == 0:
                        n_ = ts(acc[:, s, :], abuf[:, 0, :], c_, None, ALU.mult)
                    else:
                        if s == 0:
                            dve.wait_ge(sem_, count)
                        n_ = stt(acc[:, s, :], abuf[:, i % 2, :], c_, acc[:, s, :], ALU.mult, ALU.add)
                    n_.then_inc(sem_, 1)

            def gate_out(ph, r, per_r, first, used, bank, n, factor, gate_of):
                dve.wait_ge(tile_used, used)
                for q in range(NTT[ph]):
                    idx = first + q
                    dve.wait_ge(added[ph], r * per_r + (idx + 1))
                    stt(tmp[:, idx % 2, :], ps[:, bank + q, :], factor,
                        gates[:, gate_of(q), n * TILE_N:(n + 1) * TILE_N], ALU.mult, ALU.mult
                        ).then_inc(gated[ph], 1)

            def ffn(f, base, nt):
                s = F[f]
                dve.wait_ge(*((gates_in, 32) if f == 0 else (gate_set, 2)))
                gate_of = (lambda q: q // 2) if f == 0 else (lambda q: 1)

                def hidden(g, p):
                    for b in range(2):
                        dve.wait_ge(s["silu_done"], g * GROUP_FF + (2 * p + b + 1))
                        tt(hf[:, b, 0:nt], sg[:, b, 0:nt], ps[:, 4 * p + 2 + b, 0:nt], ALU.mult
                           ).then_inc(s["hf_done"], 1)
                    for b in range(2):
                        dve.wait_ge(s["hh_done"], g * GROUP_FF + (2 * p + b + 1))
                        tt(htl[:, 2 * p + b, 0:nt], hf[:, b, 0:nt], hth[:, 2 * p + b, 0:nt].bitcast(F32),
                           ALU.subtract).then_inc(s["h_ready"], 1)

                def group(r, per, g, t0, seg):
                    for j in range(GROUP_TILES):
                        split(r, per, t0 + j + AHEAD)
                        if seg is not None:
                            if j == 1:
                                dve.wait_ge(red_pe, g + 1)
                                V.tensor_copy(adac[:, :, ds(g, 1), :], ps[:, 7, 0:2 * PB].rearrange(
                                                  "p (s o b) -> p s o b", b=PB, o=1)).then_inc(red_out, 1)
                            if 1 <= j <= KT:
                                piece(j - 1, SEGMENTS[seg][2], g * (8 * KT) + 16 * ((j - 1) // 2 + 1), acc_done,
                                      acc_count(g, seg, j - 1))
                        if j in (K_TILES - 1, 2 * K_TILES - 1):
                            hidden(g, j // K_TILES)
                        elif j >= PAIRS * K_TILES and j % OUT_TILES == OUT_TILES - 1:
                            n = (j - PAIRS * K_TILES) // OUT_TILES
                            gate_out(f, g, N_OUT * NTT[f], n * NTT[f], tiles(r, per, t0 + j) + HL,
                                     4 * (n % 2), n, 0.5, gate_of)

                if f == 0:
                    for seg, (lo, hi, _) in enumerate(SEGMENTS):
                        with dve.Fori(lo, hi) as g:
                            group(g, GROUP_TILES, g, base, seg)
                else:
                    with dve.Fori(0, GROUPS - 1) as g:
                        group(g, GROUP_TILES, g, base, None)
                    group(0, 0, GROUPS - 1, base + (GROUPS - 1) * GROUP_TILES, None)

            def head_out(h, off):
                dve.wait_ge(tile_used, tiles(h, K_TILES, T_HEADS + (off + 1) * K_TILES - 1) + HL)
                V.tensor_copy(pq[:, CONV_LEFT:CONV_LEFT + SEQ], ps[:, 0, 0:SEQ]).then_inc(HS["evac_dve"], 1)
                if off:
                    dve.wait_ge(HS["act_in"], at("act_in", h, 4))
                V.tensor_copy(pz[:], ps[:, 3, 0:SEQ]).then_inc(HS["evac_dve"], 1)

            def decay_prep():
                n = [0]

                def link(i):
                    n[0] += 1
                    i.then_inc(prep_dve, 1)
                    dve.wait_ge(prep_dve, n[0])

                dve.wait_ge(ba_done, 1)
                V.tensor_copy(baT[:], ps[0:N_BA, 4, :]).then_inc(bat_set, 1)
                ba = ps[:, 5, 0:4 * N_BA].rearrange("p (t n) -> p t n", t=4)
                xg, e, r_, s2, q_, m = (sp_t[:, i] for i in range(6))
                dve.wait_ge(ba_done, 2)
                dve.wait_ge(rowc_in, 32)
                link(tt(xg, ba[:, :, 16:32], bc(rowc[:, 0, :], 4), ALU.add))
                link(stt(e, xg, -1.0, xg, ALU.mult, ALU.max))
                dve.wait_ge(prep_act, 3)
                link(ts(r_, e, 2.0, None, ALU.add))
                link(V.reciprocal(r_, r_))
                link(tt(e, e, r_, ALU.mult))
                link(tt(s2, e, e, ALU.mult))
                link(ts(q_, s2, 1.0 / 15, None, ALU.mult))
                for o_ in (13, 11, 9, 7, 5, 3):
                    link(stt(q_, q_, 1.0 / o_, s2, ALU.add, ALU.mult))
                link(stt(q_, q_, 1.0, e, ALU.add, ALU.mult))
                link(ts(m, xg, 0.0, None, ALU.max))
                link(stt(q_, q_, 2.0, m, ALU.mult, ALU.add))
                link(stt(gp[:, G], q_, -1.0, bc(rowc[:, 1, :], 4), ALU.mult, ALU.mult))
                assert n[0] == PREP_G
                dve.wait_ge(prep_pe, 1)
                dve.wait_ge(prep_act, 5)
                sums = ps[:, 6, 0:128].rearrange("p (t n) -> p t n", t=4)
                link(V.tensor_copy(gp[:, GC], sums[:, :, 0:16]))
                link(tt(gp[:, EKD], sums[:, :, 16:32], gp[:, GC], ALU.subtract))
                dve.wait_ge(prep_act, 4)
                link(stt(gp[:, NBEG], gp[:, BETA], -1.0, gp[:, EG], ALU.mult, ALU.mult))
                dve.wait_ge(prep_act, 6)

            def conv(h, off, what):
                def done(i, name):
                    i.then_inc(HS[name], 1)

                def wait(name, k):
                    dve.wait_ge(HS[name], at(name, h, PER[name] * off + k))

                n = "kvq".index(what)
                if n == 0:
                    taps = cols_c[:, 0:96].rearrange("p (a h) -> p a h", h=HEADS)
                    done(V.tensor_copy(cw[:].unsqueeze(2), taps[:, :, ds(h + off, 1)]), "cw_set")
                    wait("cw_set", 1)
                    wait("evac_act", 1)
                elif n == 1:
                    wait("evac_act", 2)
                else:
                    wait("evac_dve", 2)
                buf, dst, c_ = ((pk, kT, 1), (pv, vT, 2), (pq, qT, 0))[n]
                for j in range(CONV_W):
                    tap = cw[:, 3 * j + c_:3 * j + c_ + 1]
                    src = buf[:, j:j + SEQ] if buf is pq else buf[:, :, j:j + SEQ]
                    if j == 0:
                        i = ts(dst[:], src, tap, None, ALU.mult)
                    else:
                        wait("conv", CONV_W * n + j)
                        i = stt(dst[:], src, tap, dst[:], ALU.mult, ALU.add)
                    done(i, "conv")

            def gdn(h, point, more):
                def done(i, name):
                    i.then_inc(HS[name], 1)

                def wait(name, k):
                    dve.wait_ge(HS[name], at(name, h, k))

                def quad(bank):
                    return ps[:, bank, :].rearrange("p (q n) -> p q n", q=4)

                done(V.tensor_copy(hp[:].rearrange("p k t d -> p (k t) d"),
                                   gp[:].rearrange("p k t (d h) -> p (k t) d h", h=HEADS)[:, :, :, h]
                                   if isinstance(h, int) else
                                   gp[:].rearrange("p k t (d h) -> p (k t) d h", h=HEADS)[:, :, :, ds(h, 1)]
                                   .rearrange("p a d o -> p a (d o)")), "hp_set")
                point(0)
                point(1)
                wait("pe_ss", 1)
                done(ts(ssb[:], ps[:, 6, 0:6], EPS, None, ALU.add), "ss_sb")
                wait("rs_set", 1)
                wait("pe_k", 1)
                for q in range(4):
                    i = ts(kh[:, q, :], ps[:, 5, q * P:(q + 1) * P], rs[:, q:q + 1], None, ALU.mult)
                done(i, "kh_set")
                done(ts(rq[:], rs[:, 4:6], DK ** -0.5, None, ALU.mult), "rq_set")
                point(2)
                for d in range(2):
                    wait("pe_cum", d + 1)
                    for q in range(4):
                        i = stt(LE[:, 4 * d + q, :], ps[:, 4 + 2 * d, q * P:(q + 1) * P],
                                hp[:, GC, q, d:d + 1], mk[:, MASKED + d, :], ALU.subtract, ALU.max)
                    done(i, "dd_set")
                wait("pe_g", 1)
                for d in range(2):
                    wait("e_set", d + 1)
                    for q in range(4):
                        i = stt(AY[:, 4 * d + q, :], LE[:, 4 * d + q, :], hp[:, BETA, q, d:d + 1],
                                ps[:, 5, q * P:(q + 1) * P], ALU.mult, ALU.mult)
                    done(i, "a_set")
                wait("ei_set", 1)
                wait("pe_qk", 1)
                for d in range(2):
                    i = tt(Aq[:, 2 * d:2 * d + 2, :], Aq[:, 2 * d:2 * d + 2, :],
                           ps[:, 7, 0:2 * P].rearrange("p (q n) -> p q n", q=2), ALU.mult)
                done(i, "aq_set")
                point(3)
                for k, buf in enumerate((X, X, XT, XT)):
                    d = k % 2
                    b = slice(4 * d, 4 * d + 4)
                    if k < 2:
                        wait("m1_set", d + 1)
                    else:
                        wait("at_set", d + 1)
                        done(tt(XT[:, b, :], AT[:, b, :], level_mask(d, True, 0), ALU.mult), "mt_set")
                        wait("mt_set", d + 1)
                    done(tt(buf[:, b, :], bc(ident[:], 4), buf[:, b, :], ALU.subtract), "x1_set")
                point(4)
                last = len(LEVELS) - 1
                for l in range(last + 1):
                    for d in range(2):
                        b = slice(4 * d, 4 * d + 4)
                        m = LEVELS[l]
                        if l < last:
                            wait("pe_z", 2 * l + d + 1)
                            part = half(X[:, b, :], m, d, False)
                            done(tt(part, part, ps[:, 4 + 2 * d, 0:SEQ].rearrange("p (a m) -> p a m", m=m),
                                    ALU.subtract), "x_set")
                        wait("pe_zt", 2 * l + d + 1)
                        part = half(XT[:, b, :], m, d, True)
                        done(tt(part, part, ps[:, 5 + 2 * d, 0:SEQ].rearrange("p (a m) -> p a m", m=m),
                                ALU.subtract), "xt_set")
                wait("vb_set", 1)
                for s in range(4):
                    for d in range(2):
                        q = SCAN[d][s]
                        if s:
                            wait("pe_r", 2 * (s - 1) + d + 1)
                            done(stt(vbp[:, d, :], ps[:, 4 + 2 * d, 0:P], hp[:, NBEG, q, d:d + 1],
                                     vb[:, 4 * d + q, :], ALU.mult, ALU.add), "vbp_set")
                        if s == 2:
                            done(ts(o[:, q, :], ps[:, 5 + 2 * d, 0:P], hp[:, EG, q, d:d + 1], None,
                                    ALU.mult), "o_set")
                        if s == 3:
                            wait("o_set", 4)
                            done(stt(o[:, q, :], ps[:, 5 + 2 * d, 0:P], hp[:, EG, q, d:d + 1],
                                     o[:, q, :], ALU.mult, ALU.add), "o_set")
                    for d in range(2):
                        q = SCAN[d][s]
                        if s < 3:
                            wait("pe_kv", 2 * s + d + 1)
                            if s == 0:
                                i = V.tensor_copy(S[:, d, :], ps[:, 4 + 2 * d, 2 * P:3 * P])
                            else:
                                i = stt(S[:, d, :], S[:, d, :], hp[:, EGT, q, d:d + 1],
                                        ps[:, 4 + 2 * d, 2 * P:3 * P], ALU.mult, ALU.add)
                            done(i, "s_set")
                        if s >= 2:
                            wait("pe_av", 2 * (s - 2) + d + 1)
                            wait("o_set", 4 * (s - 2) + d + 1 if s == 2 else 6)
                            done(tt(o[:, q, :], o[:, q, :], ps[:, 5 + 2 * d, P:2 * P], ALU.add), "o_set")
                    if s < 3:
                        point(5 + s)
                if more:
                    head_out(h, 1)
                wait("o_set", 8)
                for q in range(2):
                    i = ts(o[:, q, :], o[:, q, :], rq[:, q:q + 1], None, ALU.mult)
                done(i, "osc")
                if more:
                    conv(h, 1, "k")
                wait("oss_set", 1)
                done(ts(oms[:], oss[:], 1.0 / DK, EPS, ALU.mult, ALU.add), "oms_set")
                wait("ors_set", 1)
                for q in range(2):
                    i = ts(o[:, q, :], o[:, q, :], ors[:, q:q + 1], None, ALU.mult)
                done(i, "on_set")
                if more:
                    conv(h, 1, "v")
                wait("pe_o", 1)
                wait("act_in", 4)
                done(stt(yg[:, ds(h, 1), :], ps[:, 4:5, 0:SEQ], cols_c[:, 104:105], zs[:].unsqueeze(1),
                         ALU.mult, ALU.mult), "y_done")
                if more:
                    conv(h, 1, "q")

            ada()
            split_x(0, 2)
            dve.wait_ge(x_turned, 4)
            V.memset(acc[:], 0.0).then_inc(acc_zero, 1)
            ffn(0, T_FFN1, NTOK)
            dve.wait_ge(red_pe, GROUPS + 1)
            V.tensor_copy(adac[:, 0, GROUPS, :], ps[:, 7, 0:PB]).then_inc(red_out, 1)
            dve.wait_ge(red_out, GROUPS + 1)
            for s in range(2):
                n = GROUPS if s == 0 else 2 * D // HALF
                v_ = adac[:, s, 1:1 + n, :].rearrange("p a b -> p (a b)")
                tt(v_, v_, cols_b[:, 48:48 + n * PB], ALU.add).then_inc(bias_done, 1)
            dve.wait_ge(bias_done, 2)
            scales(2, [(adac[:, s, 3:5].rearrange("p a b -> p (a b)"), 1) for s in range(2)] +
                   [(adac[:, 0, 9:11].rearrange("p a b -> p (a b)"), 2)])
            dve.wait_ge(added[0], GROUPS * N_OUT * NTT[0] + 2)
            scale(2, True)
            split_x(8, 2)
            for b_ in (pq[:, 0:CONV_LEFT], pq[:, CONV_LEFT + SEQ:], pk[:, :, 0:CONV_LEFT],
                       pk[:, :, CONV_LEFT + SEQ:], pv[:, :, 0:CONV_LEFT], pv[:, :, CONV_LEFT + SEQ:]):
                i = V.memset(b_, 0.0)
            i.then_inc(margins_set, 1)
            dve.wait_ge(margins_set, 1)
            for k in range(K_TILES):
                split(0, 0, T_HEADS + k + AHEAD)
            dve.wait_ge(ba_hi, 1)
            tt(wbal[:], wba[:], wbah[:].bitcast(F32), ALU.subtract).then_inc(ba_split, 1)
            head_out(0, 0)
            decay_prep()
            for what in "kvq":
                conv(0, 0, what)
            with dve.Fori(0, HEADS - 1) as h:
                gdn(h, lambda k: split(h, K_TILES, T_HEADS + K_TILES + k + AHEAD), True)
            gdn(HEADS - 1, lambda k: split(0, 0, T_POOL + k + AHEAD), False)
            for k in range(K_TILES):
                split(0, 0, T_POOL + K_TILES + k + AHEAD)
            dve.wait_ge(pool_pe, 1)
            for b in range(2, 4):
                V.tensor_copy(pT[:, 2 * b:2 * b + 2, :].rearrange("p a b -> p (a b)"), ps[:, 4 + b, :]
                              ).then_inc(pool_p, 1)
            dve.wait_ge(HS["y_done"], HEADS + 1)
            V.tensor_copy(xh[:, 8:16, 0:SEQ], yg[:]).then_inc(y_hi, 1)
            dve.wait_ge(y_hi, 1)
            tt(xl[:, 8:16, 0:SEQ], yg[:], xh[:, 8:16, 0:SEQ].bitcast(F32), ALU.subtract).then_inc(y_ready, 1)
            dve.wait_ge(yp_done, 1)
            V.tensor_copy(xh[:, 0:8, 0:SEQ], yp[:]).then_inc(y_hi, 1)
            dve.wait_ge(y_hi, 2)
            tt(xl[:, 0:8, 0:SEQ], yp[:], xh[:, 0:8, 0:SEQ].bitcast(F32), ALU.subtract).then_inc(y_ready, 1)
            dve.wait_ge(gate_set, 1)
            for n in range(N_OUT):
                for k in range(K_TILES):
                    split(0, 0, T_WOUT + n * K_TILES + k + AHEAD)
                    if k % 2:
                        i = (n * K_TILES + k) // 2
                        piece(i, 1, GROUPS * 8 * KT + 16 * (i // 2 + 1), acc8_done, i)
                gate_out(2, 0, 0, n * NTT[2], T_WOUT + (n + 1) * K_TILES + HL, 4 * (n % 2), n, 1.0, lambda q: 0)
            dve.wait_ge(red_pe, GROUPS + 2)
            v_ = adac[:, 0, PIECES, :]
            tt(v_, ps[:, 2, 0:PB], cols_b[:, 48 + GROUPS * PB:], ALU.add).then_inc(red_out, 1)
            dve.wait_ge(added[2], N_OUT * NTT[2] + 2)
            scale(4, False)
            split_x(16, 1)
            ffn(1, T_FFN2, SEQ)
            dve.wait_ge(fg_in, 16)
            dve.wait_ge(added[1], GROUPS * N_OUT * NTT[1] + 2)
            rstd(5)
            dve.wait_ge(rstd_done, 6)
            for t in range(2):
                stt(xn[:, t, :], h_lat[:, t, :], n_rstd[:, 0, t:t + 1], gates[:, 0, :], ALU.mult, ALU.mult
                    ).then_inc(fin_done, 1)

        @block.gpsimd
        def _(pool):
            tt = nc.gpsimd.tensor_tensor

            def rstd(c_):
                pool.wait_ge(ms_done, c_ + 1)
                s = c_ % 2 if c_ < 4 else 0
                tt(n_rstd[:, s], n_ms[:, s], mhalf[:, 0:2], ALU.pow).then_inc(rstd_done, 1)

            def add_out(ph, groups, where):
                per = N_OUT * NTT[ph]

                def blocks(g):
                    for n in range(N_OUT):
                        for q in range(NTT[ph]):
                            idx = n * NTT[ph] + q
                            pool.wait_ge(gated[ph], g * per + (idx + 1 + per))
                            dst = where[q // 2][:, q % 2, n * TILE_N:(n + 1) * TILE_N]
                            tt(dst, dst, tmp[:, idx % 2, :], ALU.add).then_inc(added[ph], 1)
                if groups == 1:
                    blocks(0)
                else:
                    with pool.Fori(0, groups) as g:
                        blocks(g)

            def gdn(h):
                def done(i, name):
                    i.then_inc(HS[name], 1)

                def wait(name, k):
                    pool.wait_ge(HS[name], at(name, h, k))

                wait("ss_sb", 1)
                done(tt(rs[:], ssb[:], mhalf[:, 0:6], ALU.pow), "rs_set")
                for d in range(2):
                    wait("e_set", d + 1)
                    i = tt(Aq[:, 2 * d:2 * d + 2, :], LE[:, 4 * d:4 * d + 2, :], bc(ident[:], 2), ALU.add)
                done(i, "ei_set")
                for d in range(2):
                    b = slice(4 * d, 4 * d + 4)
                    wait("a_set", d + 1)
                    done(tt(X[:, b, :], AY[:, b, :], level_mask(d, False, 0), ALU.mult), "m1_set")
                wait("ei_set", 1)
                for l in range(len(LEVELS)):
                    for d in range(2):
                        b = slice(4 * d, 4 * d + 4)
                        if l:
                            wait("pe_y", 2 * (l - 1) + d + 1)
                        else:
                            wait("at_set", d + 1)
                        done(tt(LE[:, b, :], AT[:, b, :], level_mask(d, True, l + 1), ALU.mult), "lt_set")
                for d in range(2):
                    wait("pe_y", 2 * len(LEVELS) - 1 + d)
                    for q in SCAN[d][:3]:
                        i = tt(LE[:, 4 * d + q, :], kh[:, q, :], hp[:, EKD, q, d:d + 1].broadcast_to([P, P]), ALU.mult)
                    done(i, "kd_set")
                wait("oms_set", 1)
                done(tt(ors[:], oms[:], mhalf[:, 0:2], ALU.pow), "ors_set")

            nc.gpsimd.memset(mhalf[:], -0.5).then_inc(half_set, 1)
            pool.wait_ge(half_set, 1)
            pool.wait_ge(x_in, 48)
            tt(h_lat[:], h_lat[:], gates[:], ALU.add).then_inc(h_set, 1)
            rstd(0)
            rstd(1)
            add_out(0, GROUPS, (h_lat, h_ctx))
            rstd(2)
            rstd(3)
            pool.wait_ge(mk_in, 16)
            with pool.Fori(0, HEADS) as h:
                gdn(h)
            add_out(2, 1, (h_lat,))
            rstd(4)
            add_out(1, GROUPS, (h_lat,))
            rstd(5)


_INS = ["x", "c", "ctx", "c_ctx", "w_ada", "b_ada", "norm_g", "w_in", "conv_w", "a_log", "dt_bias",
        "o_norm_g", "w_pool", "pool_scale", "w_out", "ffn_w_in", "ffn_w_out", "final_g"]


def kernel(**inputs):
    import concourse.bacc as bacc
    from concourse.bass_utils import run_bass_kernel_spmd

    nc = bacc.Bacc("TRN2", target_bir_lowering=False, num_devices=1)
    arrays, args = {}, []
    given = {n: np.ascontiguousarray(inputs[n]) for n in _INS}
    given.update({"const_" + n: a for n, a in host_constants().items()})
    for name, a in given.items():
        arrays[f"in_{name}"] = a
        args.append(nc.dram_tensor(f"in_{name}", a.shape, mybir.dt.from_np(a.dtype), kind="ExternalInput").ap())
    args.append(nc.dram_tensor("out_0", (1, SEQ, D), F32, kind="ExternalOutput").ap())
    build(nc, *args)
    return run_bass_kernel_spmd(nc, [arrays], core_ids=[0]).results[0]["out_0"]
```
